# Optimizing a Trainium2 kernel written in Bass

```python
import math
import jax, jax.numpy as jnp
from jax import lax
import numpy as np

D_MODEL = 1024
BATCH = 1
SEQ = 512
DEPTH = 1

MEM_LEN = 256
MLA_HEADS = 8
MLA_Q_RANK = 384
MLA_KV_RANK = 256
MLA_NOPE = 64
MLA_ROPE = 32
MLA_V = 64
Q_BLOCK = 128
RET_HEADS = 4
RET_DK = 128
RET_DV = 128
RET_CHUNK = 128
MIX_WIDTH = MLA_HEADS * MLA_V + RET_HEADS * RET_DV
IN_WIDTHS = (MLA_Q_RANK, MLA_KV_RANK, MLA_ROPE,
             RET_HEADS * RET_DK, RET_HEADS * RET_DK, RET_HEADS * RET_DV, RET_HEADS * RET_DV)
IN_WIDTH = sum(IN_WIDTHS)
IN_SPLITS = tuple(int(s) for s in np.cumsum(IN_WIDTHS)[:-1])
X_HEADS = 4
X_HEAD_DIM = D_MODEL // X_HEADS
PEER_KEYS = 128
PEER_EXPERTS = PEER_KEYS * PEER_KEYS
PEER_HEADS = 8
PEER_TOPK = 16
PEER_DKEY = 256
PEER_BLOCK = 128
ROPE_BASE = 10000.0
EPS = 1e-6
NEG = -1e30

kernel_name = "hymba_mla_retention_peer_block"

def rmsnorm(x, g):
    xf = x.astype(jnp.float32)
    y = xf * lax.rsqrt(jnp.mean(xf * xf, axis=-1, keepdims=True) + EPS)
    return (y * g.astype(jnp.float32)).astype(x.dtype)

def rope_tables(pos, dim):
    inv = 1.0 / (ROPE_BASE ** (jnp.arange(0, dim, 2, dtype=jnp.float32) / dim))
    ang = pos[:, None] * inv[None, :]
    return jnp.cos(ang), jnp.sin(ang)

def apply_rope(x, cos, sin):
    half = x.shape[-1] // 2
    c = cos[None, :, None, :].astype(x.dtype)
    s = sin[None, :, None, :].astype(x.dtype)
    x1, x2 = x[..., :half], x[..., half:]
    return jnp.concatenate([x1 * c - x2 * s, x1 * s + x2 * c], axis=-1)

def blocked_causal_attention(q, k, v, scale):
    B, S, H, dq = q.shape
    dv = v.shape[-1]
    nb = S // Q_BLOCK
    qb = q.reshape(B, nb, Q_BLOCK, H, dq).transpose(1, 0, 2, 3, 4)
    kpos = jnp.arange(S)

    def one_block(args):
        qblk, i = args
        s = jnp.einsum('bqhd,bkhd->bhqk', qblk, k).astype(jnp.float32) * scale
        qpos = i * Q_BLOCK + jnp.arange(Q_BLOCK)
        mask = kpos[None, :] <= qpos[:, None]
        s = jnp.where(mask[None, None], s, NEG)
        p = jax.nn.softmax(s, axis=-1)
        return jnp.einsum('bhqk,bkhd->bqhd', p.astype(v.dtype), v)

    out = lax.map(one_block, (qb, jnp.arange(nb)))
    return out.transpose(1, 0, 2, 3, 4).reshape(B, S, H, dv)

def chunkwise_retention(q, k, v):
    B, S, H, dk = q.shape
    dv = v.shape[-1]
    C = RET_CHUNK
    n = S // C
    log_g = jnp.log(1.0 - 2.0 ** (-5.0 - jnp.arange(H, dtype=jnp.float32)))
    idx = jnp.arange(C, dtype=jnp.float32)
    rel = idx[:, None] - idx[None, :]
    decay = jnp.where(rel[None] >= 0, jnp.exp(jnp.maximum(rel, 0.0)[None] * log_g[:, None, None]), 0.0)
    zeta = jnp.exp((C - 1 - idx)[None, :] * log_g[:, None])
    xi = jnp.exp((idx + 1)[None, :] * log_g[:, None])
    chunk_decay = jnp.exp(C * log_g)
    qc = q.reshape(B, n, C, H, dk)
    kc = k.reshape(B, n, C, H, dk)
    vc = v.reshape(B, n, C, H, dv)
    scores = jnp.einsum('bnihd,bnjhd->bnhij', qc, kc) * decay[None, None]
    inner = jnp.einsum('bnhij,bnjhe->bnihe', scores, vc)
    kz = kc * zeta.T[None, None, :, :, None]
    kv = jnp.einsum('bnjhd,bnjhe->bnhde', kz, vc)

    def step(R, kv_i):
        return R * chunk_decay[None, :, None, None] + kv_i, R

    _, R_prev = lax.scan(step, jnp.zeros((B, H, dk, dv), jnp.float32), kv.transpose(1, 0, 2, 3, 4))
    R_prev = R_prev.transpose(1, 0, 2, 3, 4)
    cross = jnp.einsum('bnihd,bnhde->bnihe', qc, R_prev) * xi.T[None, None, :, :, None]
    return (inner + cross).reshape(B, S, H, dv)

def hybrid_mixer(a, w_in, g_q_lora, w_uq, g_kv_lora, w_ukv, g_ret_gn, w_o, cos_m, sin_m, cos_r, sin_r):
    B, S, _ = a.shape
    proj = a @ w_in
    c_q, c_kv, k_pe, r_q, r_k, r_v, r_g = jnp.split(proj, IN_SPLITS, axis=-1)
    q = (rmsnorm(c_q, g_q_lora) @ w_uq).reshape(B, S, MLA_HEADS, MLA_NOPE + MLA_ROPE)
    q = jnp.concatenate([q[..., :MLA_NOPE], apply_rope(q[..., MLA_NOPE:], cos_m, sin_m)], axis=-1)
    kv = (rmsnorm(c_kv, g_kv_lora) @ w_ukv).reshape(B, S, MLA_HEADS, MLA_NOPE + MLA_V)
    k_pe = apply_rope(k_pe[:, :, None, :], cos_m, sin_m)
    k = jnp.concatenate([kv[..., :MLA_NOPE], jnp.broadcast_to(k_pe, (B, S, MLA_HEADS, MLA_ROPE))], axis=-1)
    v = kv[..., MLA_NOPE:]
    o_mla = blocked_causal_attention(q, k, v, (MLA_NOPE + MLA_ROPE) ** -0.5).reshape(B, S, MLA_HEADS * MLA_V)
    rq = apply_rope(r_q.reshape(B, S, RET_HEADS, RET_DK), cos_r, sin_r)
    rk = apply_rope(r_k.reshape(B, S, RET_HEADS, RET_DK), cos_r, sin_r) * (RET_DK ** -0.5)
    rv = r_v.reshape(B, S, RET_HEADS, RET_DV)
    o = chunkwise_retention(rq.astype(jnp.float32), rk.astype(jnp.float32), rv.astype(jnp.float32))
    mu = jnp.mean(o, axis=-1, keepdims=True)
    var = jnp.mean(jnp.square(o - mu), axis=-1, keepdims=True)
    o = ((o - mu) * lax.rsqrt(var + EPS)).reshape(B, S, RET_HEADS * RET_DV) * g_ret_gn.astype(jnp.float32)
    o_ret = (jax.nn.silu(r_g.astype(jnp.float32)) * o).astype(a.dtype)
    return jnp.concatenate([o_mla, o_ret], axis=-1) @ w_o

def memory_cross_attention(a, mem_n, w_xq, w_xkv, w_xo):
    B, S, D = a.shape
    M = mem_n.shape[1]
    q = (a @ w_xq).reshape(B, S, X_HEADS, X_HEAD_DIM)
    kv = (mem_n @ w_xkv).reshape(B, M, 2, X_HEADS, X_HEAD_DIM)
    k, v = kv[:, :, 0], kv[:, :, 1]
    s = jnp.einsum('bshd,bmhd->bhsm', q, k).astype(jnp.float32) * (X_HEAD_DIM ** -0.5)
    p = jax.nn.softmax(s, axis=-1)
    o = jnp.einsum('bhsm,bmhd->bshd', p.astype(v.dtype), v).reshape(B, S, D)
    return o @ w_xo

def peer_ffn(a, w_pq, sub_keys, u_experts, v_experts):
    B, S, D = a.shape
    T = B * S
    t = a.reshape(T, D)
    q = (t @ w_pq).reshape(T, PEER_HEADS, 2, PEER_DKEY // 2)
    s = jnp.einsum('thpd,pkd->thpk', q, sub_keys).astype(jnp.float32)
    top_s, top_i = lax.top_k(s, PEER_TOPK)
    cand = top_s[:, :, 0, :, None] + top_s[:, :, 1, None, :]
    best_s, best_c = lax.top_k(cand.reshape(T, PEER_HEADS, PEER_TOPK * PEER_TOPK), PEER_TOPK)
    i1 = jnp.take_along_axis(top_i[:, :, 0], best_c // PEER_TOPK, axis=-1)
    i2 = jnp.take_along_axis(top_i[:, :, 1], best_c % PEER_TOPK, axis=-1)
    expert = i1 * PEER_KEYS + i2
    gate = jax.nn.softmax(best_s, axis=-1)
    nb = T // PEER_BLOCK

    def one_block(args):
        tb, eb, gb = args
        u = u_experts[eb]
        act = jax.nn.gelu(jnp.einsum('thkd,td->thk', u, tb).astype(jnp.float32), approximate=False)
        w = (gb * act).astype(tb.dtype)
        return jnp.einsum('thk,thkd->td', w, v_experts[eb])

    out = lax.map(one_block, (t.reshape(nb, PEER_BLOCK, D),
                              expert.reshape(nb, PEER_BLOCK, PEER_HEADS, PEER_TOPK),
                              gate.reshape(nb, PEER_BLOCK, PEER_HEADS, PEER_TOPK)))
    return out.reshape(B, S, D)

def setup_inputs(seed: int = 0) -> dict:
    key = jax.random.key(seed)
    ks = jax.random.split(key, 24)
    f32 = jnp.float32

    def nrm(k, shape, scale):
        return jax.random.normal(k, shape, f32) * scale

    def gain(k, shape):
        return 1.0 + 0.02 * jax.random.normal(k, shape, f32)

    L = DEPTH
    return {
        "x": nrm(ks[0], (BATCH, SEQ, D_MODEL), 1.0),
        "mem": nrm(ks[1], (BATCH, MEM_LEN, D_MODEL), 1.0),
        "g_mix": gain(ks[2], (L, D_MODEL)),
        "w_in": nrm(ks[3], (L, D_MODEL, IN_WIDTH), D_MODEL ** -0.5),
        "g_q_lora": gain(ks[4], (L, MLA_Q_RANK)),
        "w_uq": nrm(ks[5], (L, MLA_Q_RANK, MLA_HEADS * (MLA_NOPE + MLA_ROPE)), MLA_Q_RANK ** -0.5),
        "g_kv_lora": gain(ks[6], (L, MLA_KV_RANK)),
        "w_ukv": nrm(ks[7], (L, MLA_KV_RANK, MLA_HEADS * (MLA_NOPE + MLA_V)), MLA_KV_RANK ** -0.5),
        "g_ret_gn": gain(ks[8], (L, RET_HEADS * RET_DV)),
        "w_o": nrm(ks[9], (L, MIX_WIDTH, D_MODEL), MIX_WIDTH ** -0.5),
        "g_xattn": gain(ks[10], (L, D_MODEL)),
        "g_mem": gain(ks[11], (L, D_MODEL)),
        "w_xq": nrm(ks[12], (L, D_MODEL, D_MODEL), D_MODEL ** -0.5),
        "w_xkv": nrm(ks[13], (L, D_MODEL, 2 * D_MODEL), D_MODEL ** -0.5),
        "w_xo": nrm(ks[14], (L, D_MODEL, D_MODEL), D_MODEL ** -0.5),
        "g_ffn": gain(ks[15], (L, D_MODEL)),
        "w_pq": nrm(ks[16], (L, D_MODEL, PEER_HEADS * PEER_DKEY), D_MODEL ** -0.5),
        "sub_keys": nrm(ks[17], (L, 2, PEER_KEYS, PEER_DKEY // 2), (PEER_DKEY // 2) ** -0.5),
        "u_experts": nrm(ks[18], (L, PEER_EXPERTS, D_MODEL), D_MODEL ** -0.5),
        "v_experts": nrm(ks[19], (L, PEER_EXPERTS, D_MODEL), PEER_HEADS ** -0.5),
        "g_final": gain(ks[20], (D_MODEL,)),
    }

def reference(x, mem, g_mix, w_in, g_q_lora, w_uq, g_kv_lora, w_ukv, g_ret_gn, w_o,
              g_xattn, g_mem, w_xq, w_xkv, w_xo, g_ffn, w_pq, sub_keys, u_experts, v_experts, g_final):
    S = x.shape[1]
    pos = jnp.arange(S, dtype=jnp.float32)
    cos_m, sin_m = rope_tables(pos, MLA_ROPE)
    cos_r, sin_r = rope_tables(pos, RET_DK)
    h = x
    for l in range(DEPTH):
        a = rmsnorm(h, g_mix[l])
        h = h + hybrid_mixer(a, w_in[l], g_q_lora[l], w_uq[l], g_kv_lora[l], w_ukv[l], g_ret_gn[l], w_o[l],
                             cos_m, sin_m, cos_r, sin_r)
        a = rmsnorm(h, g_xattn[l])
        h = h + memory_cross_attention(a, rmsnorm(mem, g_mem[l]), w_xq[l], w_xkv[l], w_xo[l])
        a = rmsnorm(h, g_ffn[l])
        h = h + peer_ffn(a, w_pq[l], sub_keys[l], u_experts[l], v_experts[l])
    return rmsnorm(h, g_final)


_drawn_inputs = setup_inputs


def setup_inputs(seed=0):
    import zlib

    import numpy as np

    out = dict(_drawn_inputs(seed))
    spreads = {}
    factors = {'g_q_lora': 6.967,
     'g_kv_lora': 5.881,
     'g_ret_gn': 3.401,
     'g_xattn': 6.751,
     'g_mem': 5.644,
     'g_final': 8.702,
     'g_ffn': 8.0}
    for name, (base, spread) in spreads.items():
        noise = np.random.default_rng([zlib.crc32(name.encode()), seed]).standard_normal(out[name].shape)
        drawn = base * np.exp(spread * noise) if base else spread * noise
        out[name] = __import__('jax').numpy.asarray(drawn.astype(out[name].dtype))
    for name, factor in factors.items():
        out[name] = (out[name] * factor).astype(out[name].dtype)
    return out
```

```python
from contextlib import ExitStack

import numpy as np

import concourse.bass as bass
from concourse import mybir

P = 128
ALU = mybir.AluOpType
ACT = mybir.ActivationFunctionType
AX = mybir.AxisListType
F32 = mybir.dt.float32
U32 = mybir.dt.uint32

SEQ, D = 512, 1024
NBLK = SEQ // P
GROUPS = ((0,), (1, 2, 3))
GMAX = max(len(g) for g in GROUPS)
DC = D // P
H, NOPE, ROPE, VD = 8, 64, 32, 64
QK = NOPE + ROPE
QR, KVR = 384, 256
RH, RD = 4, 128
MEM = 256
MT = MEM // P
XH, XD = 4, 256
PH, KEYS, TOPK = 8, 128, 16
CW = 256
W_SLOTS = 4
ROWS = 8
BANKS = 6
LAG = 2
EPS = 1e-6
NEG = -1e30
LOW = -3.0e38
MLA_SCALE = QK ** -0.5
X_SCALE = XD ** -0.5

CONST = {}
_at = 0
for _name, _n in (("ident", P), ("causal", P), ("ret_mask", P), ("iota", TOPK), ("key_decay", RH),
                  ("zeta", RH), ("xi", RH), ("xi2", RH), ("eps", 1), ("ret_cos", NBLK * 64),
                  ("ret_sin", NBLK * 64), ("mla_cos", NBLK * 16), ("mla_sin", NBLK * 16)):
    CONST[_name] = (_at, _at + _n)
    _at += _n
CONST_W = _at


def constants():
    f = np.float32
    c = np.zeros((P, CONST_W), f)

    def put(name, value):
        a, b = CONST[name]
        c[:, a:b] = value

    i = np.arange(P)
    put("ident", np.eye(P, dtype=f))
    put("causal", np.where(i[None, :] <= i[:, None], f(0), f(NEG)))
    put("ret_mask", np.where(i[None, :] >= i[:, None], f(1), f(0)))
    put("iota", np.arange(TOPK, dtype=f)[None, :])
    gamma = 1.0 - 2.0 ** (-5.0 - np.arange(RH))
    scale = RD ** -0.5
    put("key_decay", scale * gamma[None, :] ** -(i[:, None] + 1.0))
    put("zeta", scale * gamma[None, :] ** (P - 1.0 - i[:, None]))
    put("xi", gamma[None, :] ** (i[:, None] + 1.0))
    put("xi2", gamma[None, :] ** (2 * (i[:, None] + 1.0)))
    put("eps", EPS)
    pos = np.arange(SEQ, dtype=f)
    for name, dim in (("ret", RD), ("mla", ROPE)):
        inv = f(1) / (f(10000.0) ** (np.arange(0, dim, 2, dtype=f) / f(dim)))
        ang = (pos[:, None] * inv[None, :]).astype(f).reshape(NBLK, P, dim // 2).transpose(1, 0, 2)
        put(name + "_cos", np.cos(ang).reshape(P, -1))
        put(name + "_sin", np.sin(ang).reshape(P, -1))
    return c


def chunk_list():
    out = []
    for g in range(len(GROUPS)):
        out += [(g, "in", c) for c in range(3)] + [(g, "uq", 0), (g, "uq", 1), (g, "ukv", 0)]
        for h in range(RH):
            out += [(g, "qk", h), (g, "vg", h)]
        out += [(g, "o", c) for c in range(4)]
        if g == 0:
            for h in range(XH):
                out += [(g, "xk", h), (g, "xv", h)]
        out += [(g, "xq", h) for h in range(XH)] + [(g, "xo", c) for c in range(4)]
        out += [(g, "pq", h) for h in range(PH)]
    return out


def norm_list():
    out = []
    for g, blocks in enumerate(GROUPS):
        out += [("mix", b) for b in blocks]
        if g == 0:
            out += [("mem", m) for m in range(MT)]
        out += [("x", b) for b in blocks] + [("ffn", b) for b in blocks]
    return out + [("fin", b) for b in range(NBLK)]


def nth(item, b, items):
    blocks = next(g for g in GROUPS if b in g)
    return items * blocks[0] + item * len(blocks) + b - blocks[0] + 1


class Signal:

    def __init__(self, sem):
        self.sem, self.n = sem, 0


class Tile:

    def __init__(self, ap, full, free, use):
        self.ap, self.full, self.free = ap, (full, use), (free, use)


def build_trunk(nc, t, out, consts):
    chunks = chunk_list()
    chunk_no = {key: n for n, key in enumerate(chunks)}
    norms = norm_list()
    norm_no = {key: n for n, key in enumerate(norms)}

    with ExitStack() as ctx:
        def sb(name, shape, dt=F32):
            return ctx.enter_context(nc.sbuf_tensor(name, shape, dt))

        def sem(name):
            return ctx.enter_context(nc.semaphore(name))

        banks = [ctx.enter_context(nc.psum_tensor(f"bank{k}", [P, 512], F32)) for k in range(8)]

        cst = sb("cst", [P, CONST_W])
        h_sb = sb("h_sb", [P, NBLK, D])
        t_cur = sb("t_cur", [P, D])
        g_mix = sb("g_mix", [P, D])
        g_x = sb("g_x", [P, D])
        g_ffn = sb("g_ffn", [P, D])
        g_q = sb("g_q", [P, QR])
        g_kv = sb("g_kv", [P, KVR])
        g_ret = sb("g_ret", [P, RH * RD])
        w_ring = sb("w_ring", [P, W_SLOTS, DC * CW])
        rows = sb("rows", [P, ROWS, D])
        k_mla = sb("k_mla", [QK, H, SEQ])
        v_mla = sb("v_mla", [P, NBLK, H, VD])
        r_state = sb("r_state", [P, RH, RD])
        xk = sb("xk", [P, 2 * XH, MEM])
        xv = sb("xv", [P, MT, D])
        sk = sb("sk", [P, 2, KEYS])
        expert = sb("expert", [P, NBLK * PH, TOPK], U32)
        gate = sb("gate", [P, NBLK * PH, TOPK])
        stage_u = sb("stage_u", [P, TOPK], U32)
        stage_v = sb("stage_v", [P, TOPK], U32)
        dots = sb("dots", [P, TOPK])
        acts = sb("acts", [P, TOPK])
        pick_w = sb("pick_w", [P, TOPK])
        ssq = sb("ssq", [P, len(norms)])
        std = sb("std", [P, len(norms)])
        rstd = sb("rstd", [P, len(norms)])
        a_t = sb("a_t", [P, DC, GMAX * P])
        mix = sb("mix", [P, GMAX, D])
        probs = sb("probs", [P, LAG + 1, 512])
        probs_t = sb("probs_t", [P, 2, 512])
        top = sb("top", [P, LAG + 1])
        mx = sb("mx", [P, 1])
        den = sb("den", [P, 8])
        rden = sb("rden", [P, 8])
        lora = sb("lora", [P, 2, 3])
        gn = sb("gn", [P, GMAX, RH, 2])
        gn_s = sb("gn_s", [P, 4, RH])
        gn_stats = sb("gn_stats", [P, 6])
        scratch = sb("scratch", [P, 5216])

        at = [0]

        def cut(*shape):
            n = int(np.prod(shape))
            ap = scratch[:, at[0]:at[0] + n]
            at[0] += n
            assert at[0] <= 5216
            names = "abc"[:len(shape)]
            if len(shape) == 1:
                return ap
            return ap.rearrange(f"p ({' '.join(names)}) -> p {' '.join(names)}",
                                **dict(zip(names, shape)))

        mp = cut(GMAX, QR + KVR + ROPE)
        lora_t = cut(5, P)
        q_cat = cut(H, QK)
        k_cat = cut(H, QK)
        q_t = cut(H, P)
        rot_a, rot_b = probs_t[:, 0, 0:256], probs_t[:, 1, 0:256]
        kpe = sb("kpe", [P, ROPE])
        at[0] = 0
        ret_in = cut(3, 4 * RD)
        ret_qk = cut(3, 2 * RD)
        ret_qk_t = cut(3, 2 * RD)
        ret_s = cut(3, RD)
        ret_kz = cut(3, RD)
        ret_gate = cut(3, RD)
        ret_e = cut(RD)
        ret_sig = cut(RD)
        at[0] = 0
        xq_t = cut(2, 2, GMAX * P)
        rest = cut(KEYS)
        cand = cut(TOPK, TOPK)
        cand2 = cut(TOPK * TOPK)
        hit = cut(TOPK, TOPK)
        hit2 = cut(TOPK, TOPK)
        key_s = cut(2, TOPK)
        best = cut(TOPK)
        soft = cut(TOPK)
        picked = cut(2, TOPK)
        small = cut(8)
        key_i = sb("key_i", [P, 2, TOPK], U32)
        best_c = sb("best_c", [P, TOPK], U32)
        split = sb("split", [P, 2, TOPK], U32)

        def const(name):
            a, b = CONST[name]
            return cst[:, a:b]

        ident = const("ident")
        eps = const("eps")

        const_in = sem("const_in")
        gains_in = sem("gains_in")
        sub_in = sem("sub_in")
        mem_in = sem("mem_in")
        g_mem_in = sem("g_mem_in")
        g_fin_in = sem("g_fin_in")
        x_in = [sem(f"x_in{b}") for b in range(NBLK)]
        w_in_slot = [sem(f"w_in_slot{s}") for s in range(W_SLOTS)]
        row_in = [sem(f"row_in{s}") for s in range(ROWS)]
        out_done = sem("out_done")
        bank_full = [sem(f"bank_full{k}") for k in range(8)]
        bank_free = [sem(f"bank_free{k}") for k in range(8)]
        act_step = Signal(sem("act_step"))
        dve_step = Signal(sem("dve_step"))
        std_ready = Signal(sem("std_ready"))
        normed = Signal(sem("normed"))
        lora_std = Signal(sem("lora_std"))
        lora_normed = Signal(sem("lora_normed"))
        q_roped = Signal(sem("q_roped"))
        k_joined = Signal(sem("k_joined"))
        mla_top = Signal(sem("mla_top"))
        mla_out = Signal(sem("mla_out"))
        ret_roped = Signal(sem("ret_roped"))
        ret_exp = Signal(sem("ret_exp"))
        ret_gated = Signal(sem("ret_gated"))
        ret_kz_ready = Signal(sem("ret_kz_ready"))
        ret_s_ready = Signal(sem("ret_s_ready"))
        r_ready = Signal(sem("r_ready"))
        gn_var = Signal(sem("gn_var"))
        gn_std = Signal(sem("gn_std"))
        mixed = Signal(sem("mixed"))
        mix_added = Signal(sem("mix_added"))
        x_top = Signal(sem("x_top"))
        x_out = Signal(sem("x_out"))
        x_added = Signal(sem("x_added"))
        best_ready = Signal(sem("best_ready"))
        soft_ready = Signal(sem("soft_ready"))
        expert_ready = Signal(sem("expert_ready"))
        stage_step = sem("stage_step")
        row_used = sem("row_used")
        row_claimed = sem("row_claimed")
        gelu_ready = sem("gelu_ready")
        weights_ready = sem("weights_ready")
        t_ready = Signal(sem("t_ready"))
        out_ready = Signal(sem("out_ready"))

        tiles = {}
        uses = [0] * 8
        turn = [0, 0]
        chunk_freed = {}

        def tile(*name):
            return tiles[name]

        block = ctx.enter_context(nc.Block())

        @block.tensor
        def _(pe):
            def open_tile(name, long_lived=False):
                if long_lived:
                    k = BANKS + turn[1] % (8 - BANKS)
                    turn[1] += 1
                else:
                    k = turn[0] % BANKS
                    turn[0] += 1
                if uses[k]:
                    pe.wait_ge(bank_free[k], uses[k])
                uses[k] += 1
                tiles[name] = Tile(banks[k], bank_full[k], bank_free[k], uses[k])
                return tiles[name]

            def turn_over(tl, src, n, rows_out=P):
                for i in range(n):
                    ins = pe.transpose(tl.ap[0:rows_out, i * P:(i + 1) * P], src(i), ident)
                ins.then_inc(tl.full[0], 1)

            def weights(g, kind, n):
                no = chunk_no[(g, kind, n)]
                slot, use = no % W_SLOTS, no // W_SLOTS
                pe.wait_ge(w_in_slot[slot], 32 * (use + 1))
                return w_ring[:, slot, :].rearrange("p (c n) -> p c n", c=DC)

            def release(g, kind, n, tl):
                chunk_freed[(g, kind, n)] = tl.full

            def left_operand(kind, blocks, done, value):
                for j, b in enumerate(blocks):
                    pe.wait_ge(done.sem, value(b))
                    for i in range(2):
                        tl = open_tile((kind, b, i))
                        turn_over(tl, lambda c: mix[:, j, (4 * i + c) * P:(4 * i + c + 1) * P], 4)

            def rows_product(g, kind, n, width, blocks, tag, src):
                w = weights(g, kind, n)
                for j, b in enumerate(blocks):
                    if n == 0:
                        pe.wait_ge(*tile(src, b, 1).free)
                    tl = open_tile((tag, n, b))
                    for c in range(DC):
                        ins = pe.matmul(tl.ap[:, 0:width], a_t[:, c, j * P:(j + 1) * P], w[:, c, 0:width],
                                        start=c == 0, stop=c == DC - 1)
                    ins.then_inc(tl.full[0], 1)
                release(g, kind, n, tl)

            def columns_product(g, kind, n, blocks, tag, src):
                w = weights(g, kind, n)
                if n == 0:
                    for b in blocks:
                        pe.wait_ge(*tile(src, b, 1).free)
                for i in range(2):
                    tl = open_tile((tag, n, i))
                    for c in range(DC):
                        ins = pe.matmul(tl.ap[:, 0:len(blocks) * P], w[:, c, i * P:(i + 1) * P],
                                        a_t[:, c, 0:len(blocks) * P], start=c == 0, stop=c == DC - 1)
                    ins.then_inc(tl.full[0], 1)
                release(g, kind, n, tl)

            pe.wait_ge(const_in, 16)
            for g, blocks in enumerate(GROUPS):
                if g == 0:
                    pe.wait_ge(sub_in, 16)
                    tl = open_tile(("sk",))
                    turn_over(tl, lambda p: rows[:, 1, p * P:(p + 1) * P], 2)
                left_operand("mix_t", blocks, normed, lambda b: norm_no[("mix", b)] + 1)
                for c in range(3):
                    rows_product(g, "in", c, CW if c < 2 else QR + KVR + ROPE - 2 * CW, blocks, "mp", "mix_t")

                for j, b in enumerate(blocks):
                    pe.wait_ge(lora_normed.sem, b + 1)
                    for i, n in ((0, 3), (1, 2)):
                        tl = open_tile(("lora_t", b, i))
                        turn_over(tl, lambda c: mp[:, j, (3 * i + c) * P:(3 * i + c + 1) * P], n)
                    for i in range(2):
                        no = chunk_no[(g, "uq", i)]
                        pe.wait_ge(w_in_slot[no % W_SLOTS], 32 * (no // W_SLOTS + 1))
                        w = w_ring[:, no % W_SLOTS, 0:3 * 384].rearrange("p (c n) -> p c n", c=3)
                        if i == 0:
                            pe.wait_ge(*tile("lora_t", b, 0).free)
                        tl = open_tile(("q", b, i))
                        for c in range(3):
                            ins = pe.matmul(tl.ap[:, 0:384], lora_t[:, c, :], w[:, c, :], start=c == 0, stop=c == 2)
                        ins.then_inc(tl.full[0], 1)
                        release(g, "uq", i, tl)
                    no = chunk_no[(g, "ukv", 0)]
                    pe.wait_ge(w_in_slot[no % W_SLOTS], 32 * (no // W_SLOTS + 1))
                    w = w_ring[:, no % W_SLOTS, :].rearrange("p (c n) -> p c n", c=2)
                    pe.wait_ge(*tile("lora_t", b, 1).free)
                    for i in range(2):
                        tl = open_tile(("kv", b, i))
                        for c in range(2):
                            ins = pe.matmul(tl.ap[:, :], lora_t[:, 3 + c, :], w[:, c, i * 512:(i + 1) * 512],
                                            start=c == 0, stop=c == 1)
                        ins.then_inc(tl.full[0], 1)
                    release(g, "ukv", 0, tl)
                    pe.wait_ge(k_joined.sem, b + 1)
                    for i in range(2):
                        tl = open_tile(("k_t", b, i))
                        turn_over(tl, lambda c: k_cat[:, 4 * i + c, :], 4, QK)
                    pe.wait_ge(q_roped.sem, b + 1)
                    for i in range(2):
                        tl = open_tile(("q_t", b, i))
                        turn_over(tl, lambda c: q_cat[:, 4 * i + c, :], 4, QK)
                    to = open_tile(("o", b), long_lived=True)
                    for h in range(H + LAG):
                        if h < H:
                            if h % 4 == 0:
                                pe.wait_ge(*tile("k_t", b, h // 4).free)
                                pe.wait_ge(*tile("q_t", b, h // 4).free)
                            tl = open_tile(("s", b, h))
                            pe.matmul(tl.ap[:, 0:(b + 1) * P], q_t[0:QK, h, :], k_mla[:, h, 0:(b + 1) * P],
                                      start=True, stop=True).then_inc(tl.full[0], 1)
                        if h >= LAG:
                            i = h - LAG
                            pe.wait_ge(*tile("s", b, i).free)
                            tl = open_tile(("p_t", b, i))
                            turn_over(tl, lambda c: probs[:, i % (LAG + 1), c * P:(c + 1) * P], b + 1)
                            pe.wait_ge(*tl.free)
                            for c in range(b + 1):
                                ins = pe.matmul(to.ap[:, i * VD:(i + 1) * VD], probs_t[:, i % 2, c * P:(c + 1) * P],
                                                v_mla[:, c, i, :], start=c == 0, stop=c == b)
                            if i == H - 1:
                                ins.then_inc(to.full[0], 1)

                items = [(h, b) for h in range(RH) for b in blocks]
                for n in range(len(items) + 2):
                    if n < len(items):
                        h, b = items[n]
                        j = b - blocks[0]
                        tl = open_tile(("r", h, b))
                        for half, kind in enumerate(("qk", "vg")):
                            w = weights(g, kind, h)
                            for c in range(DC):
                                ins = pe.matmul(tl.ap[:, half * CW:(half + 1) * CW], a_t[:, c, j * P:(j + 1) * P],
                                                w[:, c, :], start=c == 0, stop=c == DC - 1)
                            release(g, kind, h, tl)
                        ins.then_inc(tl.full[0], 1)
                    if 1 <= n <= len(items):
                        h, b = items[n - 1]
                        k = (n - 1) % 3
                        pe.wait_ge(ret_roped.sem, nth(h, b, RH))
                        tl = open_tile(("r_t", h, b))
                        turn_over(tl, lambda i: ret_qk[:, k, i * RD:(i + 1) * RD], 2)
                    if n >= 2:
                        h, b = items[n - 2]
                        k = (n - 2) % 3
                        pe.wait_ge(ret_s_ready.sem, nth(h, b, RH))
                        tl = open_tile(("r_o", h, b))
                        ins = pe.matmul(tl.ap[:, 0:RD], ret_s[:, k, :], ret_in[:, k, 2 * RD:3 * RD],
                                        start=True, stop=b == 0)
                        if b:
                            pe.wait_ge(r_ready.sem, r_count(h, b - 1))
                            ins = pe.matmul(tl.ap[:, 0:RD], ret_qk_t[:, k, 0:RD], r_state[:, h, :],
                                            start=False, stop=True)
                        ins.then_inc(tl.full[0], 1)
                        if b < NBLK - 1:
                            pe.wait_ge(ret_kz_ready.sem, nth(h, b, RH))
                            tl = open_tile(("r_kv", h, b))
                            pe.matmul(tl.ap[:, 0:RD], ret_kz[:, k, :], ret_in[:, k, 2 * RD:3 * RD],
                                      start=True, stop=True).then_inc(tl.full[0], 1)
                    if 1 <= n <= len(items):
                        h, b = items[n - 1]
                        k = (n - 1) % 3
                        pe.wait_ge(*tile("r_t", h, b).free)
                        tl = open_tile(("r_s", h, b))
                        pe.matmul(tl.ap[:, 0:P], ret_qk_t[:, k, RD:2 * RD], ret_qk_t[:, k, 0:RD],
                                  start=True, stop=True).then_inc(tl.full[0], 1)

                left_operand("out_t", blocks, mixed, lambda b: b + 1)
                for c in range(4):
                    rows_product(g, "o", c, CW, blocks, "wo", "out_t")

                if g == 0:
                    for m in range(MT):
                        pe.wait_ge(normed.sem, norm_no[("mem", m)] + 1)
                        for i in range(2):
                            tl = open_tile(("mem_t", m, i))
                            turn_over(tl, lambda c: mix[:, 1 + m, (4 * i + c) * P:(4 * i + c + 1) * P], 4)
                    for m in range(MT):
                        pe.wait_ge(*tile("mem_t", m, 1).free)
                    for h in range(XH):
                        w = weights(g, "xk", h)
                        for i in range(2):
                            tl = open_tile(("xk", h, i))
                            for c in range(DC):
                                ins = pe.matmul(tl.ap[:, 0:MEM], w[:, c, i * P:(i + 1) * P], a_t[:, c, P:P + MEM],
                                                start=c == 0, stop=c == DC - 1)
                            ins.then_inc(tl.full[0], 1)
                        release(g, "xk", h, tl)
                        w = weights(g, "xv", h)
                        for m in range(MT):
                            tl = open_tile(("xv", h, m))
                            for c in range(DC):
                                ins = pe.matmul(tl.ap[:, 0:CW], a_t[:, c, (1 + m) * P:(2 + m) * P], w[:, c, :],
                                                start=c == 0, stop=c == DC - 1)
                            ins.then_inc(tl.full[0], 1)
                        release(g, "xv", h, tl)

                left_operand("x_t", blocks, normed, lambda b: norm_no[("x", b)] + 1)
                items = [(h, b) for h in range(XH) for b in blocks]
                for n in range(len(items) + LAG):
                    if n < len(items):
                        h, b = items[n]
                        j = b - blocks[0]
                        if j == 0:
                            columns_product(g, "xq", h, blocks, ("xq", g), "x_t")
                            pe.wait_ge(*tile(("xq", g), h, 0).free)
                            pe.wait_ge(*tile(("xq", g), h, 1).free)
                        tl = open_tile(("xs", h, b))
                        for i in range(2):
                            ins = pe.matmul(tl.ap[:, 0:MEM], xq_t[:, h % 2, i, j * P:(j + 1) * P], xk[:, 2 * h + i, :],
                                            start=i == 0, stop=i == 1)
                        ins.then_inc(tl.full[0], 1)
                    if n >= LAG:
                        i = n - LAG
                        h, b = items[i]
                        pe.wait_ge(*tile("xs", h, b).free)
                        tl = open_tile(("xp_t", h, b))
                        turn_over(tl, lambda c: probs[:, i % (LAG + 1), c * P:(c + 1) * P], MT)
                        pe.wait_ge(*tl.free)
                        tl = open_tile(("xo", h, b))
                        for m in range(MT):
                            ins = pe.matmul(tl.ap[:, 0:XD], probs_t[:, i % 2, m * P:(m + 1) * P],
                                            xv[:, m, h * XD:(h + 1) * XD], start=m == 0, stop=m == MT - 1)
                        ins.then_inc(tl.full[0], 1)
                left_operand("xo_t", blocks, x_out, lambda b: nth(XH - 1, b, XH))
                for c in range(4):
                    rows_product(g, "xo", c, CW, blocks, "wxo", "xo_t")

                left_operand("f_t", blocks, normed, lambda b: norm_no[("ffn", b)] + 1)
                for h in range(PH + 1):
                    if h < PH:
                        columns_product(g, "pq", h, blocks, ("pq", g), "f_t")
                    if h >= 1:
                        for i in range(2):
                            pe.wait_ge(*tile(("pq", g), h - 1, i).free)
                        for j, b in enumerate(blocks):
                            tl = open_tile(("ps", h - 1, b))
                            for i in range(2):
                                ins = pe.matmul(tl.ap[:, i * KEYS:(i + 1) * KEYS],
                                                xq_t[:, (h - 1) % 2, i, j * P:(j + 1) * P], sk[:, i, :],
                                                start=True, stop=True)
                            ins.then_inc(tl.full[0], 1)

        @block.sync
        def _(sp):
            def rows_of(gain):
                return gain.rearrange("(a n) -> a n", a=1)

            sp.dma_start(h_sb[:, 0, :], t["x"][0, 0:P, :]).then_inc(x_in[0], 16)
            sp.dma_start(cst[:, :], consts).then_inc(const_in, 16)

            def gain(dst, src):
                sp.dma_start(dst, src.partition_broadcast(P)).then_inc(gains_in, 16)

            gain(g_mix[:, :], t["g_mix"][0])

            def load_chunk(no):
                g, kind, n = chunks[no]
                slot = no % W_SLOTS
                if no >= W_SLOTS:
                    sp.wait_ge(*chunk_freed[chunks[no - W_SLOTS]])
                dst = w_ring[:, slot, :].rearrange("p (c n) -> p c n", c=DC)
                if kind == "uq":
                    w = t["w_uq"][0].rearrange("(c p) n -> p c n", p=P)
                    dst = w_ring[:, slot, 0:3 * 384].rearrange("p (c n) -> p c n", c=3)
                    parts = [(dst[:, 0:1, :], w[:, 0:1, n * 384:(n + 1) * 384]),
                             (dst[:, 1:3, :], w[:, 1:3, n * 384:(n + 1) * 384])]
                elif kind == "ukv":
                    w = t["w_ukv"][0].rearrange("(c p) n -> p c n", p=P)
                    dst = w_ring[:, slot, :].rearrange("p (c n) -> p c n", c=2)
                    parts = [(dst[:, i, :], w[:, i, :]) for i in range(2)]
                elif kind in ("qk", "vg"):
                    w = t["w_in"][0].rearrange("(c p) n -> p c n", p=P)
                    first = QR + KVR + ROPE + (0 if kind == "qk" else 2 * RH * RD) + n * RD
                    parts = [(dst[:, :, i * RD:(i + 1) * RD],
                              w[:, :, first + i * RH * RD:first + i * RH * RD + RD]) for i in range(2)]
                else:
                    name, first, width = {
                        "in": ("w_in", n * CW, min(CW, QR + KVR + ROPE - n * CW)),
                        "o": ("w_o", n * CW, CW), "xk": ("w_xkv", n * CW, CW),
                        "xv": ("w_xkv", D + n * CW, CW), "xq": ("w_xq", n * CW, CW),
                        "xo": ("w_xo", n * CW, CW), "pq": ("w_pq", n * CW, CW)}[kind]
                    w = t[name][0].rearrange("(c p) n -> p c n", p=P)
                    parts = [(dst[:, i:i + 4, 0:width], w[:, i:i + 4, first:first + width]) for i in (0, 4)]
                for d, s in parts:
                    sp.dma_start(d, s).then_inc(w_in_slot[slot], 16)

            for no in range(W_SLOTS):
                load_chunk(no)
            for m in range(MT):
                sp.dma_start(mix[:, 1 + m, :], t["mem"][0, m * P:(m + 1) * P, :]).then_inc(mem_in, 16)
            sp.dma_start(t_cur[:, :], t["g_mem"][0].partition_broadcast(P)).then_inc(g_mem_in, 16)
            sp.dma_start(rows[:, 1, 0:2 * P].rearrange("k (p d) -> k p d", p=2),
                         t["sub_keys"][0].rearrange("p k d -> k p d")).then_inc(sub_in, 16)
            gain(g_q[:, :], t["g_q_lora"][0])
            gain(g_kv[:, :], t["g_kv_lora"][0])
            gain(g_ret[:, :], t["g_ret_gn"][0])
            gain(g_x[:, :], t["g_xattn"][0])
            gain(g_ffn[:, :], t["g_ffn"][0])
            for b in range(1, NBLK):
                sp.dma_start(h_sb[:, b, :], t["x"][0, b * P:(b + 1) * P, :]).then_inc(x_in[b], 16)
            for no in range(W_SLOTS, len(chunks)):
                load_chunk(no)
            sp.wait_ge(normed.sem, norm_no[("mix", NBLK - 1)] + 1)
            sp.dma_start(g_mix[:, :], t["g_final"].partition_broadcast(P)).then_inc(g_fin_in, 16)
            for b in range(NBLK):
                sp.wait_ge(out_ready.sem, b + 1)
                sp.dma_start(out[0, b * P:(b + 1) * P, :], rows[:, b, :]).then_inc(out_done, 16)
            sp.wait_ge(out_done, 16 * NBLK)

        @block.scalar
        def _(act):
            def link(ins, sig=act_step):
                ins.then_inc(sig.sem, 1)
                sig.n += 1
                act.wait_ge(sig.sem, sig.n)

            def empty(tl, dst, src):
                nc.scalar.activation(dst, src, ACT.Copy).then_inc(tl.free[0], 1)
                act.wait_ge(*tl.free)

            def square_root(kind, b, src, junk):
                n = norm_no[(kind, b)]
                link(nc.scalar.activation(junk, src, ACT.Square, accum_out=ssq[:, n:n + 1]))
                link(nc.scalar.activation(std[:, n:n + 1], ssq[:, n:n + 1], ACT.Sqrt, bias=eps, scale=1.0 / D),
                     std_ready)

            def left_operand(kind, blocks):
                for j, b in enumerate(blocks):
                    for i in range(2):
                        tl = tile(kind, b, i)
                        act.wait_ge(*tl.full)
                        empty(tl, a_t[:, 4 * i:4 * i + 4, j * P:(j + 1) * P],
                              tl.ap[:, :].rearrange("p (c n) -> p c n", c=4))

            def gelu(n):
                act.wait_ge(row_used, ROWS + n * 2 * TOPK + TOPK)
                nc.scalar.activation(acts[:, :], dots[:, :], ACT.Gelu).then_inc(gelu_ready, 1)
                act.wait_ge(gelu_ready, n + 1)

            act.wait_ge(const_in, 16)
            for g, blocks in enumerate(GROUPS):
                nb = len(blocks)
                for j, b in enumerate(blocks):
                    act.wait_ge(x_in[b], 16)
                    if g:
                        act.wait_ge(*tile("f_t", GROUPS[g - 1][-1], 1).full)
                    square_root("mix", b, h_sb[:, b, :], mix[:, j, :])
                if g == 0:
                    act.wait_ge(mem_in, 16 * MT)
                    for m in range(MT):
                        square_root("mem", m, mix[:, 1 + m, :], rows[:, 0, :])
                    act.wait_ge(*tile("sk").full)
                    empty(tile("sk"), sk[:, :, :], tile("sk").ap[:, 0:2 * P].rearrange("p (c n) -> p c n", c=2))
                left_operand("mix_t", blocks)
                if g:
                    act.wait_ge(expert_ready.sem, nth(PH - 1, GROUPS[g - 1][-1], PH))
                for c in range(3):
                    for j, b in enumerate(blocks):
                        tl = tile("mp", c, b)
                        w = min(CW, QR + KVR + ROPE - c * CW)
                        act.wait_ge(*tl.full)
                        empty(tl, mp[:, j, c * CW:c * CW + w], tl.ap[:, 0:w])

                for j, b in enumerate(blocks):
                    if b:
                        act.wait_ge(q_roped.sem, b)
                    link(nc.scalar.activation(probs[:, 0, 0:QR], mp[:, j, 0:QR], ACT.Square,
                                              accum_out=lora[:, 0, 0:1]))
                    link(nc.scalar.activation(probs[:, 0, 0:KVR], mp[:, j, QR:QR + KVR], ACT.Square,
                                              accum_out=lora[:, 1, 0:1]))
                    link(nc.scalar.activation(lora[:, 0, 1:2], lora[:, 0, 0:1], ACT.Sqrt, bias=eps, scale=1.0 / QR))
                    link(nc.scalar.activation(lora[:, 1, 1:2], lora[:, 1, 0:1], ACT.Sqrt, bias=eps, scale=1.0 / KVR),
                         lora_std)
                    for i, n in ((0, 3), (1, 2)):
                        tl = tile("lora_t", b, i)
                        act.wait_ge(*tl.full)
                        empty(tl, lora_t[:, 3 * i:3 * i + n, :],
                              tl.ap[:, 0:n * P].rearrange("p (c n) -> p c n", c=n))
                    for i in range(2):
                        tl = tile("q", b, i)
                        act.wait_ge(*tl.full)
                        empty(tl, q_cat[:, 4 * i:4 * i + 4, :], tl.ap[:, 0:4 * QK].rearrange("p (c n) -> p c n", c=4))
                    for i in range(2):
                        tl = tile("kv", b, i)
                        kv = tl.ap[:, :].rearrange("p (c n) -> p c n", c=4)
                        act.wait_ge(*tl.full)
                        link(nc.scalar.activation(k_cat[:, 4 * i:4 * i + 4, 0:NOPE], kv[:, :, 0:NOPE], ACT.Copy))
                        empty(tl, v_mla[:, b, 4 * i:4 * i + 4, :], kv[:, :, NOPE:NOPE + VD])
                    for i in range(2):
                        tl = tile("k_t", b, i)
                        act.wait_ge(*tl.full)
                        empty(tl, k_mla[:, 4 * i:4 * i + 4, b * P:(b + 1) * P],
                              tl.ap[0:QK, :].rearrange("p (c n) -> p c n", c=4))
                    for i in range(2):
                        tl = tile("q_t", b, i)
                        act.wait_ge(*tl.full)
                        empty(tl, q_t[0:QK, 4 * i:4 * i + 4, :], tl.ap[0:QK, :].rearrange("p (c n) -> p c n", c=4))
                    if b:
                        act.wait_ge(mla_out.sem, b)
                    for h in range(H + LAG):
                        if h < H:
                            tl = tile("s", b, h)
                            act.wait_ge(mla_top.sem, b * H + h + 1)
                            nc.scalar.activation(probs[:, h % (LAG + 1), 0:(b + 1) * P], tl.ap[:, 0:(b + 1) * P],
                                                 ACT.Exp, bias=top[:, h % (LAG + 1):h % (LAG + 1) + 1],
                                                 scale=MLA_SCALE, accum_out=den[:, h:h + 1]).then_inc(tl.free[0], 1)
                            act.wait_ge(*tl.free)
                        if h >= LAG:
                            i = h - LAG
                            tl = tile("p_t", b, i)
                            act.wait_ge(*tl.full)
                            empty(tl, probs_t[:, i % 2, 0:(b + 1) * P], tl.ap[:, 0:(b + 1) * P])

                act.wait_ge(mla_out.sem, blocks[-1] + 1)
                items = [(h, b) for h in range(RH) for b in blocks]
                for n in range(len(items) + 1):
                    if n < len(items):
                        h, b = items[n]
                        k = n % 3
                        tl = tile("r", h, b)
                        act.wait_ge(*tl.full)
                        if n >= 3:
                            act.wait_ge(ret_gated.sem, nth(*items[n - 3], RH))
                        empty(tl, ret_in[:, k, :], tl.ap[:, :])
                        if n >= 1:
                            act.wait_ge(ret_gated.sem, nth(*items[n - 1], RH))
                        link(nc.scalar.activation(ret_e, ret_in[:, k, 3 * RD:], ACT.Exp, scale=-1.0), ret_exp)
                    if n >= 1:
                        h, b = items[n - 1]
                        k = (n - 1) % 3
                        act.wait_ge(ret_roped.sem, nth(h, b, RH))
                        z = CONST["zeta"][0] + h
                        link(nc.scalar.activation(ret_kz[:, k, :], ret_qk[:, k, RD:], ACT.Copy,
                                                  scale=cst[:, z:z + 1]), ret_kz_ready)
                        tl = tile("r_t", h, b)
                        act.wait_ge(*tl.full)
                        empty(tl, ret_qk_t[:, k, :], tl.ap[:, 0:2 * RD])
                for j, b in enumerate(blocks):
                    act.wait_ge(gn_var.sem, b + 1)
                    link(nc.scalar.activation(gn_s[:, 1, :], gn_s[:, 0, :], ACT.Sqrt, bias=eps), gn_std)

                left_operand("out_t", blocks)
                if g == 0:
                    for m in range(MT):
                        for i in range(2):
                            tl = tile("mem_t", m, i)
                            act.wait_ge(*tl.full)
                            empty(tl, a_t[:, 4 * i:4 * i + 4, (1 + m) * P:(2 + m) * P],
                                  tl.ap[:, :].rearrange("p (c n) -> p c n", c=4))
                for j, b in enumerate(blocks):
                    act.wait_ge(mix_added.sem, nth(3, b, 4))
                    act.wait_ge(*tile("out_t", b, 1).full)
                    square_root("x", b, h_sb[:, b, :], mix[:, j, :])
                if g == 0:
                    for h in range(XH):
                        for i in range(2):
                            tl = tile("xk", h, i)
                            act.wait_ge(*tl.full)
                            empty(tl, xk[:, 2 * h + i, :], tl.ap[:, 0:MEM])
                        for m in range(MT):
                            tl = tile("xv", h, m)
                            act.wait_ge(*tl.full)
                            empty(tl, xv[:, m, h * XD:(h + 1) * XD], tl.ap[:, 0:XD])

                left_operand("x_t", blocks)
                items = [(h, b) for h in range(XH) for b in blocks]
                for n in range(len(items) + LAG):
                    if n < len(items):
                        h, b = items[n]
                        if b == blocks[0]:
                            for i in range(2):
                                tl = tile(("xq", g), h, i)
                                act.wait_ge(*tl.full)
                                empty(tl, xq_t[:, h % 2, i, 0:nb * P], tl.ap[:, 0:nb * P])
                        tl = tile("xs", h, b)
                        k = n % (LAG + 1)
                        act.wait_ge(x_top.sem, nth(h, b, XH))
                        nc.scalar.activation(probs[:, k, 0:MEM], tl.ap[:, 0:MEM], ACT.Exp, bias=top[:, k:k + 1],
                                             scale=X_SCALE, accum_out=den[:, k:k + 1]).then_inc(tl.free[0], 1)
                        act.wait_ge(*tl.free)
                    if n >= LAG:
                        h, b = items[n - LAG]
                        tl = tile("xp_t", h, b)
                        act.wait_ge(*tl.full)
                        empty(tl, probs_t[:, (n - LAG) % 2, 0:MEM], tl.ap[:, 0:MEM])
                        act.wait_ge(x_out.sem, nth(h, b, XH))
                left_operand("xo_t", blocks)
                for j, b in enumerate(blocks):
                    act.wait_ge(x_added.sem, nth(3, b, 4))
                    act.wait_ge(*tile("xo_t", b, 1).full)
                    square_root("ffn", b, h_sb[:, b, :], mix[:, j, :])

                left_operand("f_t", blocks)
                for h in range(PH + 1):
                    if h < PH:
                        for i in range(2):
                            tl = tile(("pq", g), h, i)
                            act.wait_ge(*tl.full)
                            empty(tl, xq_t[:, h % 2, i, 0:nb * P], tl.ap[:, 0:nb * P])
                    if h >= 1:
                        for b in blocks:
                            act.wait_ge(best_ready.sem, nth(h - 1, b, PH))
                            link(nc.scalar.activation(soft, best, ACT.Exp, bias=small[:, 0:1],
                                                      accum_out=small[:, 1:2]), soft_ready)

            with act.Fori(0, NBLK * PH) as n:
                gelu(n)
            for b in range(NBLK):
                act.wait_ge(weights_ready, NBLK * PH)
                act.wait_ge(row_used, ROWS + 2 * TOPK * PH * NBLK)
                square_root("fin", b, h_sb[:, b, :], mix[:, 0, :])

        @block.vector
        def _(dve):
            def link(ins, sig=dve_step):
                ins.then_inc(sig.sem, 1)
                sig.n += 1
                dve.wait_ge(sig.sem, sig.n)

            def last_read(ins, tl):
                ins.then_inc(tl.free[0], 1)
                dve.wait_ge(*tl.free)

            def spread(ap, *shape):
                return ap.to_broadcast([P, *shape])

            def norm(kind, b, src, dst, gain):
                n = norm_no[(kind, b)]
                dve.wait_ge(std_ready.sem, n + 1)
                link(nc.vector.reciprocal(rstd[:, n:n + 1], std[:, n:n + 1]))
                nc.vector.scalar_tensor_tensor(dst, src, rstd[:, n:n + 1], gain, ALU.mult, ALU.mult)\
                    .then_inc(normed.sem, 1)
                dve.wait_ge(normed.sem, n + 1)

            def rotate(x, dst, cos, sin, n, half, sig):
                a = rot_a[:, 0:n * 2 * half].rearrange("p (n t f) -> p n t f", n=n, t=2)
                b = rot_b[:, 0:n * 2 * half].rearrange("p (n t f) -> p n t f", n=n, t=2)
                c4 = cos.unsqueeze(1).unsqueeze(1).to_broadcast([P, n, 2, half])
                s4 = sin.unsqueeze(1).unsqueeze(1).to_broadcast([P, n, 2, half])
                link(nc.vector.tensor_tensor(a, x, c4, ALU.mult))
                link(nc.vector.tensor_tensor(b, x, s4, ALU.mult))
                link(nc.vector.tensor_tensor(dst[:, :, 0, :], a[:, :, 0, :], b[:, :, 1, :], ALU.subtract))
                link(nc.vector.tensor_tensor(dst[:, :, 1, :], b[:, :, 0, :], a[:, :, 1, :], ALU.add), sig)

            def add_product(tag, blocks, sig):
                for c in range(4):
                    for b in blocks:
                        tl = tile(tag, c, b)
                        dve.wait_ge(*tl.full)
                        hb = h_sb[:, b, c * CW:(c + 1) * CW]
                        last_read(nc.vector.tensor_tensor(hb, hb, tl.ap[:, 0:CW], ALU.add), tl)
                        if c == 3:
                            pass
                        dve.sem_inc(sig.sem, 1)
                        sig.n += 1

            def expert_head(n, b):
                used = ROWS + n * (2 * TOPK)
                for k in range(TOPK):
                    s = k % ROWS
                    dve.wait_ge(row_in[s], n * (32 * TOPK // ROWS) + 16 * (k // ROWS + 1))
                    nc.vector.tensor_tensor_reduce(out=rows[:, s, :], in0=rows[:, s, :], in1=t_cur[:, :], scale=1.0,
                                                   scalar=0.0, op0=ALU.mult, op1=ALU.add,
                                                   accum_out=dots[:, k:k + 1]).then_inc(row_used, 1)
                dve.wait_ge(gelu_ready, n + 1)
                nc.vector.tensor_tensor(pick_w[:, :], acts[:, :], gate[:, bass.ds(n, 1), :].rearrange("p a k -> p (a k)")
                                        if not isinstance(n, int) else gate[:, n, :], ALU.mult)\
                    .then_inc(weights_ready, 1)
                dve.wait_ge(weights_ready, n + 1)
                for k in range(TOPK):
                    s = k % ROWS
                    dve.wait_ge(row_in[s], n * (32 * TOPK // ROWS) + 16 * (TOPK // ROWS + k // ROWS + 1))
                    nc.vector.scalar_tensor_tensor(h_sb[:, b, :], rows[:, s, :], pick_w[:, k:k + 1], h_sb[:, b, :],
                                                   ALU.mult, ALU.add).then_inc(row_used, 1)
                    dve.wait_ge(row_used, used + TOPK + k + 1)

            def expert_tokens(b):
                n = norm_no[("ffn", b)]
                link(nc.vector.scalar_tensor_tensor(t_cur[:, :], h_sb[:, b, :], rstd[:, n:n + 1], g_ffn[:, :],
                                                    ALU.mult, ALU.mult), t_ready)

            def choose(h, b):
                tl = tile("ps", h, b)
                dve.wait_ge(*tl.full)
                for p in range(2):
                    s = tl.ap[:, p * KEYS:(p + 1) * KEYS]
                    link(nc.vector.max(key_s[:, p, 0:8], s))
                    link(nc.vector.match_replace(rest, key_s[:, p, 0:8], s, LOW))
                    link(nc.vector.max(key_s[:, p, 8:16], rest))
                    link(nc.vector.max_index(key_i[:, p, 8:16], key_s[:, p, 8:16], rest))
                    ins = nc.vector.max_index(key_i[:, p, 0:8], key_s[:, p, 0:8], s)
                    if p == 0:
                        link(ins)
                    else:
                        last_read(ins, tl)
                link(nc.vector.tensor_tensor(cand, key_s[:, 0, :].unsqueeze(2).to_broadcast([P, TOPK, TOPK]),
                                             key_s[:, 1, :].unsqueeze(1).to_broadcast([P, TOPK, TOPK]), ALU.add))
                pairs = cand.rearrange("p a b -> p (a b)")
                link(nc.vector.max(best[:, 0:8], pairs))
                link(nc.vector.match_replace(cand2, best[:, 0:8], pairs, LOW))
                link(nc.vector.max(best[:, 8:16], cand2))
                link(nc.vector.tensor_scalar(small[:, 0:1], best[:, 0:1], -1.0, None, ALU.mult), best_ready)
                link(nc.vector.max_index(best_c[:, 0:8], best[:, 0:8], pairs))
                link(nc.vector.max_index(best_c[:, 8:16], best[:, 8:16], cand2))
                link(nc.vector.tensor_scalar(split[:, 0, :], best_c[:, :], 4, None, ALU.logical_shift_right))
                link(nc.vector.tensor_scalar(split[:, 1, :], best_c[:, :], 15, None, ALU.bitwise_and))
                for p in range(2):
                    link(nc.vector.tensor_tensor(hit, split[:, p, :].unsqueeze(2).to_broadcast([P, TOPK, TOPK]),
                                                 const("iota").unsqueeze(1).to_broadcast([P, TOPK, TOPK]),
                                                 ALU.is_equal))
                    link(nc.vector.tensor_tensor(hit2, hit, key_i[:, p, :].unsqueeze(1).to_broadcast([P, TOPK, TOPK]),
                                                 ALU.mult))
                    link(nc.vector.tensor_reduce(picked[:, p, :], hit2, AX.X, ALU.add))
                dve.wait_ge(soft_ready.sem, nth(h, b, PH))
                link(nc.vector.reciprocal(small[:, 2:3], small[:, 1:2]))
                link(nc.vector.tensor_scalar(gate[:, b * PH + h, :], soft, small[:, 2:3], None, ALU.mult))
                link(nc.vector.scalar_tensor_tensor(expert[:, b * PH + h, :], picked[:, 0, :], float(KEYS),
                                                    picked[:, 1, :], ALU.mult, ALU.add), expert_ready)

            dve.sem_inc(row_used, ROWS)
            dve.wait_ge(const_in, 16)
            for g, blocks in enumerate(GROUPS):
                nb = len(blocks)
                if g == 0:
                    dve.wait_ge(gains_in, 16 * 6)
                for j, b in enumerate(blocks):
                    norm("mix", b, h_sb[:, b, :], mix[:, j, :], g_mix[:, :])
                if g == 0:
                    dve.wait_ge(g_mem_in, 16)
                    for m in range(MT):
                        norm("mem", m, mix[:, 1 + m, :], mix[:, 1 + m, :], t_cur[:, :])

                for j, b in enumerate(blocks):
                    dve.wait_ge(lora_std.sem, b + 1)
                    link(nc.vector.reciprocal(lora[:, :, 2], lora[:, :, 1]))
                    link(nc.vector.scalar_tensor_tensor(mp[:, j, 0:QR], mp[:, j, 0:QR], lora[:, 0, 2:3], g_q[:, :],
                                                        ALU.mult, ALU.mult))
                    kv = mp[:, j, QR:QR + KVR]
                    link(nc.vector.scalar_tensor_tensor(kv, kv, lora[:, 1, 2:3], g_kv[:, :], ALU.mult, ALU.mult),
                         lora_normed)
                    cos = const("mla_cos")[:, b * 16:(b + 1) * 16]
                    sin = const("mla_sin")[:, b * 16:(b + 1) * 16]
                    rotate(mp[:, j, QR + KVR:].rearrange("p (n t f) -> p n t f", n=1, t=2),
                           kpe[:, :].rearrange("p (n t f) -> p n t f", n=1, t=2), cos, sin, 1, 16, dve_step)
                    dve.wait_ge(*tile("kv", b, 1).free)
                    link(nc.vector.tensor_copy(k_cat[:, :, NOPE:],
                                               kpe[:, :].unsqueeze(1).to_broadcast([P, H, ROPE])), k_joined)
                    qr = q_cat[:, :, NOPE:].rearrange("p n (t f) -> p n t f", t=2)
                    rotate(qr, qr, cos, sin, H, 16, q_roped)
                    for h in range(H):
                        tl = tile("s", b, h)
                        k = h % (LAG + 1)
                        dve.wait_ge(*tl.full)
                        diag = tl.ap[:, b * P:(b + 1) * P]
                        link(nc.vector.tensor_tensor(diag, diag, const("causal"), ALU.add))
                        link(nc.vector.tensor_reduce(mx[:, :], tl.ap[:, 0:(b + 1) * P], AX.X, ALU.max))
                        if h > LAG:
                            dve.wait_ge(*tile("s", b, h - LAG - 1).free)
                        link(nc.vector.tensor_scalar(top[:, k:k + 1], mx[:, :], -MLA_SCALE, None, ALU.mult), mla_top)
                    to = tile("o", b)
                    dve.wait_ge(*to.full)
                    link(nc.vector.reciprocal(rden[:, :], den[:, :]))
                    last_read(nc.vector.tensor_tensor(
                        mix[:, j, 0:H * VD].rearrange("p (h d) -> p h d", h=H),
                        to.ap[:, :].rearrange("p (h d) -> p h d", h=H),
                        rden[:, :].unsqueeze(2).to_broadcast([P, H, VD]), ALU.mult), to)
                    dve.sem_inc(mla_out.sem, 1)
                    mla_out.n += 1

                items = [(h, b) for h in range(RH) for b in blocks]
                for n in range(len(items) + 2):
                    if n < len(items):
                        h, b = items[n]
                        k = n % 3
                        dve.wait_ge(*tile("r", h, b).free)
                        rotate(ret_in[:, k, 0:2 * RD].rearrange("p (n t f) -> p n t f", n=2, t=2),
                               ret_qk[:, k, :].rearrange("p (n t f) -> p n t f", n=2, t=2),
                               const("ret_cos")[:, b * 64:(b + 1) * 64], const("ret_sin")[:, b * 64:(b + 1) * 64],
                               2, 64, ret_roped)
                        dve.wait_ge(ret_exp.sem, nth(h, b, RH))
                        link(nc.vector.tensor_scalar(ret_sig, ret_e, 1.0, None, ALU.add))
                        link(nc.vector.reciprocal(ret_sig, ret_sig))
                        link(nc.vector.tensor_tensor(ret_sig, ret_sig, ret_in[:, k, 3 * RD:], ALU.mult))
                        link(nc.vector.tensor_tensor(ret_gate[:, k, :], ret_sig, g_ret[:, h * RD:(h + 1) * RD],
                                                     ALU.mult), ret_gated)
                    if n >= 2:
                        h, b = items[n - 2]
                        k = (n - 2) % 3
                        j = b - blocks[0]
                        tl = tile("r_o", h, b)
                        dve.wait_ge(*tl.full)
                        link(nc.vector.bn_stats(gn_stats[:, :], tl.ap[:, 0:RD]))
                        link(nc.vector.bn_aggr(gn[:, j, h, :], gn_stats[:, :]))
                        last_read(nc.vector.scalar_tensor_tensor(
                            mix[:, j, H * VD + h * RD:H * VD + (h + 1) * RD], tl.ap[:, 0:RD], gn[:, j, h, 0:1],
                            ret_gate[:, k, :], ALU.subtract, ALU.mult), tl)
                        if b < NBLK - 1:
                            tl = tile("r_kv", h, b)
                            dve.wait_ge(*tl.full)
                            if b == 0:
                                ins = nc.vector.tensor_copy(r_state[:, h, :], tl.ap[:, 0:RD])
                            else:
                                ins = nc.vector.scalar_tensor_tensor(
                                    r_state[:, h, :], r_state[:, h, :], float((1.0 - 2.0 ** (-5.0 - h)) ** P),
                                    tl.ap[:, 0:RD], ALU.mult, ALU.add)
                            last_read(ins, tl)
                            dve.sem_inc(r_ready.sem, 1)
                            r_ready.n += 1
                    if 1 <= n <= len(items):
                        h, b = items[n - 1]
                        k = (n - 1) % 3
                        tl = tile("r_s", h, b)
                        dve.wait_ge(*tl.full)
                        z = CONST["key_decay"][0] + h
                        last_read(nc.vector.scalar_tensor_tensor(ret_s[:, k, :], tl.ap[:, 0:P], cst[:, z:z + 1],
                                                                 const("ret_mask"), ALU.mult, ALU.mult), tl)
                        dve.sem_inc(ret_s_ready.sem, 1)
                        ret_s_ready.n += 1
                for j, b in enumerate(blocks):
                    link(nc.vector.tensor_tensor(gn_s[:, 0, :], gn[:, j, :, 1], const("xi2"), ALU.mult), gn_var)
                    dve.wait_ge(gn_std.sem, b + 1)
                    link(nc.vector.reciprocal(gn_s[:, 2, :], gn_s[:, 1, :]))
                    link(nc.vector.tensor_tensor(gn_s[:, 3, :], gn_s[:, 2, :], const("xi"), ALU.mult))
                    o = mix[:, j, H * VD:].rearrange("p (h d) -> p h d", h=RH)
                    link(nc.vector.tensor_tensor(o, o, gn_s[:, 3, :].unsqueeze(2).to_broadcast([P, RH, RD]),
                                                 ALU.mult), mixed)
                add_product("wo", blocks, mix_added)

                for j, b in enumerate(blocks):
                    norm("x", b, h_sb[:, b, :], mix[:, j, :], g_x[:, :])
                for j, b in enumerate(blocks):
                    dve.wait_ge(*tile("x_t", b, 1).full)
                items = [(h, b) for h in range(XH) for b in blocks]
                for n in range(len(items) + LAG):
                    if n < len(items):
                        h, b = items[n]
                        k = n % (LAG + 1)
                        tl = tile("xs", h, b)
                        dve.wait_ge(*tl.full)
                        link(nc.vector.tensor_reduce(mx[:, :], tl.ap[:, 0:MEM], AX.X, ALU.max))
                        link(nc.vector.tensor_scalar(top[:, k:k + 1], mx[:, :], -X_SCALE, None, ALU.mult), x_top)
                    if n >= LAG:
                        h, b = items[n - LAG]
                        k = (n - LAG) % (LAG + 1)
                        j = b - blocks[0]
                        tl = tile("xo", h, b)
                        dve.wait_ge(*tl.full)
                        link(nc.vector.reciprocal(rden[:, k:k + 1], den[:, k:k + 1]))
                        last_read(nc.vector.tensor_scalar(mix[:, j, h * XD:(h + 1) * XD], tl.ap[:, 0:XD],
                                                          rden[:, k:k + 1], None, ALU.mult), tl)
                        dve.sem_inc(x_out.sem, 1)
                        x_out.n += 1
                add_product("wxo", blocks, x_added)

                for j, b in enumerate(blocks):
                    norm("ffn", b, h_sb[:, b, :], mix[:, j, :], g_ffn[:, :])
                for h in range(PH):
                    for b in blocks:
                        choose(h, b)

            for b in range(NBLK):
                expert_tokens(b)
                with dve.Fori(b * PH, (b + 1) * PH) as n:
                    expert_head(n, b)
            dve.wait_ge(g_fin_in, 16)
            for b in range(NBLK):
                norm("fin", b, h_sb[:, b, :], rows[:, b, :], g_mix[:, :])
                dve.sem_inc(out_ready.sem, 1)

        @block.gpsimd
        def _(pool):
            def gathers(n):
                for kind, (stage, table) in enumerate(((stage_u, t["u_experts"]), (stage_v, t["v_experts"]))):
                    nc.gpsimd.tensor_copy(stage[:, :], expert[:, bass.ds(n, 1), :].rearrange("p a k -> p (a k)"))\
                        .then_inc(stage_step, 1)
                    pool.wait_ge(stage_step, 2 * n + kind + 1)
                    for k in range(TOPK):
                        s = k % ROWS
                        pool.wait_ge(row_used, n * 2 * TOPK + kind * TOPK + k + 1)
                        pool.sem_inc(row_claimed, 1)
                        nc.gpsimd.indirect_dma_start(
                            rows[:, s, :], None, table[0],
                            bass.IndirectOffsetOnAxis(ap=stage[:, k:k + 1], axis=0)).then_inc(row_in[s], 16)

            first = len(GROUPS[0]) * PH
            with pool.Fori(0, first) as n:
                pool.wait_ge(expert_ready.sem, n + 1)
                gathers(n)
            pool.wait_ge(expert_ready.sem, NBLK * PH)
            with pool.Fori(first, NBLK * PH) as n:
                gathers(n)


def r_count(h, b):
    n = 0
    for blocks in GROUPS:
        for hh in range(RH):
            for bb in blocks:
                if bb < NBLK - 1:
                    n += 1
                    if (hh, bb) == (h, b):
                        return n
    raise ValueError


_INS = ["x", "mem", "g_mix", "w_in", "g_q_lora", "w_uq", "g_kv_lora", "w_ukv", "g_ret_gn", "w_o", "g_xattn", "g_mem",
        "w_xq", "w_xkv", "w_xo", "g_ffn", "w_pq", "sub_keys", "u_experts", "v_experts", "g_final"]


def kernel(**inputs):
    import concourse.bacc as bacc
    from concourse.bass_utils import run_bass_kernel_spmd

    nc = bacc.Bacc("TRN2", target_bir_lowering=False, num_devices=1)
    arrays, t = {}, {}
    for name in _INS:
        a = np.ascontiguousarray(inputs[name])
        arrays[f"in_{name}"] = a
        t[name] = nc.dram_tensor(f"in_{name}", a.shape, mybir.dt.from_np(a.dtype), kind="ExternalInput").ap()
    arrays["in_consts"] = constants()
    consts = nc.dram_tensor("in_consts", (P, CONST_W), F32, kind="ExternalInput").ap()
    out = nc.dram_tensor("out_0", (1, SEQ, D), F32, kind="ExternalOutput").ap()
    build_trunk(nc, t, out, consts)
    r = run_bass_kernel_spmd(nc, [arrays], core_ids=[0])
    return r.results[0]["out_0"]
```

```python
from contextlib import ExitStack

import numpy as np

import concourse.bass as bass
from concourse import mybir

P = 128
ALU = mybir.AluOpType
ACT = mybir.ActivationFunctionType
AX = mybir.AxisListType
F32 = mybir.dt.float32
U32 = mybir.dt.uint32

SEQ, D = 512, 1024
NBLK = SEQ // P
GROUPS = ((0,), (1,), (2, 3))
GMAX = max(len(g) for g in GROUPS)
DC = D // P
H, NOPE, ROPE, VD = 8, 64, 32, 64
QK = NOPE + ROPE
QR, KVR = 384, 256
RH, RD = 4, 128
MEM = 256
MT = MEM // P
XH, XD = 4, 256
PH, KEYS, TOPK = 8, 128, 16
CW = 256
W_SLOTS = 4
ROWS = 12
UNROLL = 3
BANKS = 5
SUM_BANK = 6
HEAD_STEPS = 2 * TOPK + 1
DVE_ROWS = TOPK + TOPK // 2
PE_ROWS = TOPK // 2
DIAGS = 8
EARLY = 4
LAG = 2
SCRATCH = 4544
EPS = 1e-6
NEG = -1e30
LOW = -3.0e38
MLA_SCALE = QK ** -0.5
X_SCALE = XD ** -0.5

CONST = {}
_at = 0
for _name, _n in (("ident", P), ("causal", P), ("ret_mask", P), ("iota", TOPK), ("key_decay", RH),
                  ("zeta", RH), ("xi", RH), ("xi2", RH), ("eps", 1), ("ret_cos", NBLK * 64),
                  ("ret_sin", NBLK * 64), ("mla_cos", NBLK * 16), ("mla_sin", NBLK * 16)):
    CONST[_name] = (_at, _at + _n)
    _at += _n
CONST_W = _at


GAINS = {"g_mix": DC, "g_mem": DC, "g_xattn": DC, "g_ffn": DC, "g_q_lora": QR // P, "g_kv_lora": KVR // P,
         "g_ret_gn": RH * RD // P}


def constants():
    f = np.float32
    c = np.zeros((P, CONST_W), f)

    def put(name, value):
        a, b = CONST[name]
        c[:, a:b] = value

    i = np.arange(P)
    put("ident", np.eye(P, dtype=f))
    put("causal", np.where(i[None, :] <= i[:, None], f(0), f(NEG)))
    put("ret_mask", np.where(i[None, :] >= i[:, None], f(1), f(0)))
    put("iota", np.arange(TOPK, dtype=f)[None, :])
    gamma = 1.0 - 2.0 ** (-5.0 - np.arange(RH))
    scale = RD ** -0.5
    put("key_decay", scale * gamma[None, :] ** -(i[:, None] + 1.0))
    put("zeta", scale * gamma[None, :] ** (P - 1.0 - i[:, None]))
    put("xi", gamma[None, :] ** (i[:, None] + 1.0))
    put("xi2", gamma[None, :] ** (2 * (i[:, None] + 1.0)))
    put("eps", EPS)
    pos = np.arange(SEQ, dtype=f)
    for name, dim in (("ret", RD), ("mla", ROPE)):
        inv = f(1) / (f(10000.0) ** (np.arange(0, dim, 2, dtype=f) / f(dim)))
        ang = (pos[:, None] * inv[None, :]).astype(f).reshape(NBLK, P, dim // 2).transpose(1, 0, 2)
        put(name + "_cos", np.cos(ang).reshape(P, -1))
        put(name + "_sin", np.sin(ang).reshape(P, -1))
    return c


def chunk_list():
    out = []
    for g in range(len(GROUPS)):
        out += [(g, "in", c) for c in range(3)] + [(g, "uq", 0), (g, "uq", 1), (g, "ukv", 0)]
        if g == 0:
            for h in range(XH):
                out += [(g, "xk", h), (g, "xv", h)]
        for h in range(RH):
            out += [(g, "qk", h), (g, "vg", h)]
        out += [(g, "o", c) for c in range(4)]
        out += [(g, "xq", h) for h in range(XH)] + [(g, "xo", c) for c in range(4)]
        out += [(g, "pq", h) for h in range(PH)]
    return out


def norm_list():
    out = []
    for g, blocks in enumerate(GROUPS):
        out += [("mix", b) for b in blocks]
        if g == 0:
            out += [("mem", m) for m in range(MT)]
        out += [("x", b) for b in blocks] + [("ffn", b) for b in blocks]
    return out + [("fin", b) for b in range(NBLK)]


def nth(item, b, items):
    blocks = next(g for g in GROUPS if b in g)
    return items * blocks[0] + item * len(blocks) + b - blocks[0] + 1


SHARES = {"mla": 1.0, "ret": 2.0, "add": 1.3, "x": 2.0, "choose": 0.67}


assert UNROLL * 2 * TOPK % ROWS == 0


class Head:

    def __init__(self, at, turn=0):
        self.at, self.turn = at, turn

    def times(self, per_head, more):
        return self.turn * (UNROLL * per_head) + (self.at * per_head + more)

    def slot(self, row):
        return (self.at * 2 * TOPK + row) % ROWS

    def landed(self, row):
        return self.turn * (16 * UNROLL * 2 * TOPK // ROWS) + 16 * ((self.at * 2 * TOPK + row) // ROWS + 1)


def in_loops(eng, first, last, body):
    turns = (last - first) // UNROLL
    if turns > 1:
        with eng.Fori(0, turns) as turn:
            for u in range(UNROLL):
                body(Head(first + u, turn))
        first += turns * UNROLL
    for n in range(first, last):
        body(Head(n))


def step_plan():
    plan = {}
    places = []
    for g, blocks in enumerate(GROUPS):
        nb = len(blocks)
        kinds = (["mla"] * (H * nb) + ["ret"] * (RH * nb) + ["add"] * 4 + ["x"] * (XH * nb) + ["add"] * 4
                 + ["choose"] * (3 * PH * nb))
        places.append([(g, i, SHARES[k] * (nb if k == "add" else 1)) for i, k in enumerate(kinds)])
        for i in range(len(kinds)):
            plan[(g, i)] = range(0)
    for g, blocks in enumerate(GROUPS):
        chosen = 3 * PH * len(blocks)
        where = places[g][-chosen + 3 * len(blocks):]
        heads = PH * len(blocks)
        if g + 1 < len(GROUPS):
            where = where + places[g + 1][:-3 * PH * len(GROUPS[g + 1])]
        else:
            heads = EARLY
        total = heads * HEAD_STEPS
        first = blocks[0] * PH * HEAD_STEPS
        whole, seen, done = sum(w for *_, w in where), 0.0, 0
        for gg, i, w in where:
            seen += w
            upto = round(total * seen / whole)
            plan[(gg, i)] = range(first + done, first + upto)
            done = upto
    return plan





class Signal:

    def __init__(self, sem):
        self.sem, self.n = sem, 0


class Tile:

    def __init__(self, ap, full, free, use):
        self.ap, self.full, self.free = ap, (full, use), (free, use)


def build_trunk(nc, t, out, consts):
    chunks = chunk_list()
    chunk_no = {key: n for n, key in enumerate(chunks)}
    norms = norm_list()
    norm_no = {key: n for n, key in enumerate(norms)}
    plan = step_plan()
    loop_from = GROUPS[-1][0] * PH + EARLY

    with ExitStack() as ctx:
        def sb(name, shape, dt=F32):
            return ctx.enter_context(nc.sbuf_tensor(name, shape, dt))

        def sem(name):
            return ctx.enter_context(nc.semaphore(name))

        banks = [ctx.enter_context(nc.psum_tensor(f"bank{k}", [P, 512], F32)) for k in range(8)]

        cst = sb("cst", [P, CONST_W])
        h_sb = sb("h_sb", [P, NBLK, D])
        t_cur = sb("t_cur", [P, D])
        g_rows = sb("g_rows", [P, D])
        g_cols = sb("g_cols", [P, len(GAINS), DC])
        w_ring = sb("w_ring", [P, W_SLOTS, DC * CW])
        rows = sb("rows", [P, ROWS, D])
        k_mla = sb("k_mla", [QK, H, SEQ])
        v_mla = sb("v_mla", [P, NBLK, H, VD])
        r_state = sb("r_state", [P, RH, RD])
        xk = sb("xk", [P, 2 * XH, MEM])
        xv = sb("xv", [P, MT, D])
        sk = sb("sk", [P, 2, KEYS])
        expert = sb("expert", [P, NBLK * PH, TOPK], U32)
        gate = sb("gate", [P, NBLK * PH, TOPK])
        mem_rows = rows[:, 2:2 + MT, :]
        mem_t = rows[:, 2 + MT:4 + MT, :].rearrange("p a (c n) -> p (a c) n", n=MEM)
        stage_u = sb("stage_u", [P, TOPK], U32)
        stage_v = sb("stage_v", [P, TOPK], U32)
        diag = sb("diag", [P, DIAGS, P])
        dots = sb("dots", [P, TOPK])
        acts = sb("acts", [P, TOPK])
        pick_w = sb("pick_w", [P, TOPK])
        ssq = sb("ssq", [P, len(norms)])
        std = sb("std", [P, len(norms)])
        rstd = sb("rstd", [P, len(norms)])
        a_t = sb("a_t", [P, DC, GMAX * P])
        mix = sb("mix", [P, GMAX, D])
        probs = sb("probs", [P, LAG + 1, 512])
        probs_t = sb("probs_t", [P, 2, 512])
        top = sb("top", [P, LAG + 1])
        mx = sb("mx", [P, 1])
        den = sb("den", [P, 8])
        rden = sb("rden", [P, 8])
        lora = sb("lora", [P, 2, 3])
        gn = sb("gn", [P, GMAX, RH, 2])
        gn_s = sb("gn_s", [P, 4, RH])
        gn_stats = sb("gn_stats", [P, 6])
        scratch = sb("scratch", [P, SCRATCH])

        at = [0]

        def cut(*shape):
            n = int(np.prod(shape))
            ap = scratch[:, at[0]:at[0] + n]
            at[0] += n
            assert at[0] <= SCRATCH
            names = "abc"[:len(shape)]
            if len(shape) == 1:
                return ap
            return ap.rearrange(f"p ({' '.join(names)}) -> p {' '.join(names)}",
                                **dict(zip(names, shape)))

        mp = cut(GMAX, QR + KVR + ROPE)
        lora_t = cut(5, P)
        q_cat = cut(H, QK)
        k_cat = cut(H, QK)
        q_t = cut(H, P)
        rot_a, rot_b = probs_t[:, 0, 0:256], probs_t[:, 1, 0:256]
        kpe = sb("kpe", [P, ROPE])
        at[0] = 0
        ret_in = cut(3, 4 * RD)
        ret_qk = cut(3, 2 * RD)
        ret_qk_t = cut(3, 2 * RD)
        ret_s = cut(3, RD)
        ret_kz = cut(3, RD)
        ret_gate = cut(3, RD)
        ret_e = cut(RD)
        ret_sig = cut(RD)
        at[0] = 0
        xq_t = cut(2, 2, GMAX * P)
        rest = cut(2, KEYS)
        cand = cut(TOPK, TOPK)
        cand2 = cut(TOPK * TOPK)
        hit = cut(2, TOPK, TOPK)
        hit2 = cut(2, TOPK, TOPK)
        key_s = cut(2, TOPK)
        best = cut(TOPK)
        soft = cut(TOPK)
        picked = cut(2, TOPK)
        small = cut(8)
        key_i = sb("key_i", [P, 2, TOPK], U32)
        best_c = sb("best_c", [P, TOPK], U32)
        split = sb("split", [P, 2, TOPK], U32)

        def const(name):
            a, b = CONST[name]
            return cst[:, a:b]

        ident = const("ident")
        eps = const("eps")

        const_in = sem("const_in")
        gains_in = sem("gains_in")
        sub_in = sem("sub_in")
        mem_in = sem("mem_in")
        g_rows_in = sem("g_rows_in")
        x_in = [sem(f"x_in{b}") for b in range(NBLK)]
        w_in_slot = [sem(f"w_in_slot{s}") for s in range(W_SLOTS)]
        row_in = [sem(f"row_in{s}") for s in range(ROWS)]
        out_done = sem("out_done")
        bank_full = [sem(f"bank_full{k}") for k in range(8)]
        bank_free = [sem(f"bank_free{k}") for k in range(8)]
        act_step = Signal(sem("act_step"))
        dve_step = Signal(sem("dve_step"))
        std_ready = Signal(sem("std_ready"))
        normed = Signal(sem("normed"))
        lora_std = Signal(sem("lora_std"))
        lora_normed = Signal(sem("lora_normed"))
        q_roped = Signal(sem("q_roped"))
        k_joined = Signal(sem("k_joined"))
        mla_top = Signal(sem("mla_top"))
        mla_out = Signal(sem("mla_out"))
        ret_roped = Signal(sem("ret_roped"))
        ret_exp = Signal(sem("ret_exp"))
        ret_gated = Signal(sem("ret_gated"))
        ret_kz_ready = Signal(sem("ret_kz_ready"))
        ret_s_ready = Signal(sem("ret_s_ready"))
        r_ready = Signal(sem("r_ready"))
        gn_var = Signal(sem("gn_var"))
        gn_std = Signal(sem("gn_std"))
        mixed = Signal(sem("mixed"))
        mix_added = Signal(sem("mix_added"))
        x_top = Signal(sem("x_top"))
        x_out = Signal(sem("x_out"))
        x_added = Signal(sem("x_added"))
        best_ready = Signal(sem("best_ready"))
        soft_ready = Signal(sem("soft_ready"))
        expert_ready = Signal(sem("expert_ready"))
        stage_step = sem("stage_step")
        dve_used = sem("dve_used")
        pe_used = sem("pe_used")
        diag_ready = sem("diag_ready")
        sum_taken = Signal(sem("sum_taken"))
        row_claimed = sem("row_claimed")
        gelu_ready = sem("gelu_ready")
        weights_ready = sem("weights_ready")
        t_ready = Signal(sem("t_ready"))
        out_ready = Signal(sem("out_ready"))

        tiles = {}
        uses = [0] * 8
        turn = [0]
        chunk_freed = {}

        def tile(*name):
            return tiles[name]

        block = ctx.enter_context(nc.Block())

        @block.tensor
        def _(pe):
            def open_tile(name, long_lived=False):
                if long_lived:
                    k = BANKS
                else:
                    k = turn[0] % BANKS
                    turn[0] += 1
                if uses[k]:
                    pe.wait_ge(bank_free[k], uses[k])
                uses[k] += 1
                tiles[name] = Tile(banks[k], bank_full[k], bank_free[k], uses[k])
                return tiles[name]

            def expert_step(head, step, start=False, stop=False):
                k = step - TOPK - 1
                if k < 0 or k % 2 == 0:
                    return
                s = head.slot(TOPK + k)
                pe.wait_ge(diag_ready, head.times(PE_ROWS, k // 2 + 1))
                pe.wait_ge(row_in[s], head.landed(TOPK + k))
                for i in range(2):
                    ins = pe.matmul(banks[SUM_BANK + i][:, :], diag[:, k // 2, :],
                                    rows[:, s, i * 512:(i + 1) * 512], start=start, stop=stop)
                ins.then_inc(pe_used, 1)

            place = [0]
            later = []

            def experts(steps):
                for at_step in steps:
                    n, step = divmod(at_step, HEAD_STEPS)
                    start = n % PH == 0 and step == TOPK + 2
                    if start and n:
                        pe.wait_ge(sum_taken.sem, n // PH)
                    expert_step(Head(n), step, start, n % PH == PH - 1 and step == 2 * TOPK)

            def hook(g):
                experts(later)
                later[:] = plan[(g, place[0])]
                place[0] = place[0] + 1 if (g, place[0] + 1) in plan else 0

            def turn_over(tl, src, n, rows_out=P):
                for i in range(n):
                    ins = pe.transpose(tl.ap[0:rows_out, i * P:(i + 1) * P], src(i), ident)
                ins.then_inc(tl.full[0], 1)

            def weights(g, kind, n):
                no = chunk_no[(g, kind, n)]
                slot, use = no % W_SLOTS, no // W_SLOTS
                pe.wait_ge(w_in_slot[slot], 32 * (use + 1))
                return w_ring[:, slot, :].rearrange("p (c n) -> p c n", c=DC)

            def release(g, kind, n, tl):
                chunk_freed[(g, kind, n)] = tl.full

            def left_operand(kind, blocks, done, value):
                for j, b in enumerate(blocks):
                    pe.wait_ge(done.sem, value(b))
                    for i in range(2):
                        tl = open_tile((kind, b, i))
                        turn_over(tl, lambda c: mix[:, j, (4 * i + c) * P:(4 * i + c + 1) * P], 4)

            def rows_product(g, kind, n, width, blocks, tag, src):
                w = weights(g, kind, n)
                for j, b in enumerate(blocks):
                    if n == 0:
                        pe.wait_ge(*tile(src, b, 1).free)
                    tl = open_tile((tag, n, b))
                    for c in range(DC):
                        ins = pe.matmul(tl.ap[:, 0:width], a_t[:, c, j * P:(j + 1) * P], w[:, c, 0:width],
                                        start=c == 0, stop=c == DC - 1)
                    ins.then_inc(tl.full[0], 1)
                release(g, kind, n, tl)

            def columns_product(g, kind, n, blocks, tag, src):
                w = weights(g, kind, n)
                if n == 0:
                    for b in blocks:
                        pe.wait_ge(*tile(src, b, 1).free)
                for i in range(2):
                    tl = open_tile((tag, n, i))
                    for c in range(DC):
                        ins = pe.matmul(tl.ap[:, 0:len(blocks) * P], w[:, c, i * P:(i + 1) * P],
                                        a_t[:, c, 0:len(blocks) * P], start=c == 0, stop=c == DC - 1)
                    ins.then_inc(tl.full[0], 1)
                release(g, kind, n, tl)

            def memory_product(n):
                h = n // 2
                if n == 0:
                    for m in range(MT):
                        pe.wait_ge(*tile("mem_t", m, 1).free)
                if n % 2 == 0:
                    w = weights(0, "xk", h)
                    for i in range(2):
                        tl = open_tile(("xk", h, i))
                        for c in range(DC):
                            ins = pe.matmul(tl.ap[:, 0:MEM], w[:, c, i * P:(i + 1) * P], mem_t[:, c, :],
                                            start=c == 0, stop=c == DC - 1)
                        ins.then_inc(tl.full[0], 1)
                    release(0, "xk", h, tl)
                else:
                    w = weights(0, "xv", h)
                    for m in range(MT):
                        tl = open_tile(("xv", h, m))
                        for c in range(DC):
                            ins = pe.matmul(tl.ap[:, 0:CW], mem_t[:, c, m * P:(m + 1) * P], w[:, c, :],
                                            start=c == 0, stop=c == DC - 1)
                        ins.then_inc(tl.full[0], 1)
                    release(0, "xv", h, tl)

            pe.wait_ge(const_in, 16)
            for g, blocks in enumerate(GROUPS):
                if g == 0:
                    pe.wait_ge(sub_in, 16)
                    tl = open_tile(("sk",))
                    turn_over(tl, lambda p: rows[:, 1, p * P:(p + 1) * P], 2)
                left_operand("mix_t", blocks, normed, lambda b: norm_no[("mix", b)] + 1)
                for c in range(3):
                    rows_product(g, "in", c, CW if c < 2 else QR + KVR + ROPE - 2 * CW, blocks, "mp", "mix_t")

                if g == 0:
                    for m in range(MT):
                        pe.wait_ge(normed.sem, norm_no[("mem", m)] + 1)
                        for i in range(2):
                            tl = open_tile(("mem_t", m, i))
                            turn_over(tl, lambda c: mem_rows[:, m, (4 * i + c) * P:(4 * i + c + 1) * P], 4)

                for j, b in enumerate(blocks):
                    pe.wait_ge(lora_normed.sem, b + 1)
                    for i, n in ((0, 3), (1, 2)):
                        tl = open_tile(("lora_t", b, i))
                        turn_over(tl, lambda c: mp[:, j, (3 * i + c) * P:(3 * i + c + 1) * P], n)
                    for i in range(2):
                        no = chunk_no[(g, "uq", i)]
                        pe.wait_ge(w_in_slot[no % W_SLOTS], 32 * (no // W_SLOTS + 1))
                        w = w_ring[:, no % W_SLOTS, 0:3 * 384].rearrange("p (c n) -> p c n", c=3)
                        if i == 0:
                            pe.wait_ge(*tile("lora_t", b, 0).free)
                        tl = open_tile(("q", b, i))
                        for c in range(3):
                            ins = pe.matmul(tl.ap[:, 0:384], lora_t[:, c, :], w[:, c, :], start=c == 0, stop=c == 2)
                        ins.then_inc(tl.full[0], 1)
                        release(g, "uq", i, tl)
                    no = chunk_no[(g, "ukv", 0)]
                    pe.wait_ge(w_in_slot[no % W_SLOTS], 32 * (no // W_SLOTS + 1))
                    w = w_ring[:, no % W_SLOTS, :].rearrange("p (c n) -> p c n", c=2)
                    pe.wait_ge(*tile("lora_t", b, 1).free)
                    for i in range(2):
                        tl = open_tile(("kv", b, i))
                        for c in range(2):
                            ins = pe.matmul(tl.ap[:, :], lora_t[:, 3 + c, :], w[:, c, i * 512:(i + 1) * 512],
                                            start=c == 0, stop=c == 1)
                        ins.then_inc(tl.full[0], 1)
                    release(g, "ukv", 0, tl)
                    pe.wait_ge(k_joined.sem, b + 1)
                    for i in range(2):
                        tl = open_tile(("k_t", b, i))
                        turn_over(tl, lambda c: k_cat[:, 4 * i + c, :], 4, QK)
                    pe.wait_ge(q_roped.sem, b + 1)
                    for i in range(2):
                        tl = open_tile(("q_t", b, i))
                        turn_over(tl, lambda c: q_cat[:, 4 * i + c, :], 4, QK)
                    to = open_tile(("o", b), long_lived=True)
                    for h in range(H + LAG):
                        if h < H:
                            if h % 4 == 0:
                                pe.wait_ge(*tile("k_t", b, h // 4).free)
                                pe.wait_ge(*tile("q_t", b, h // 4).free)
                            tl = open_tile(("s", b, h))
                            pe.matmul(tl.ap[:, 0:(b + 1) * P], q_t[0:QK, h, :], k_mla[:, h, 0:(b + 1) * P],
                                      start=True, stop=True).then_inc(tl.full[0], 1)
                        if h >= LAG:
                            i = h - LAG
                            pe.wait_ge(*tile("s", b, i).free)
                            tl = open_tile(("p_t", b, i))
                            turn_over(tl, lambda c: probs[:, i % (LAG + 1), c * P:(c + 1) * P], b + 1)
                            pe.wait_ge(*tl.free)
                            for c in range(b + 1):
                                ins = pe.matmul(to.ap[:, i * VD:(i + 1) * VD], probs_t[:, i % 2, c * P:(c + 1) * P],
                                                v_mla[:, c, i, :], start=c == 0, stop=c == b)
                            if i == H - 1:
                                ins.then_inc(to.full[0], 1)
                        if g == 0 and h < 2 * XH:
                            memory_product(h)
                        if h < H:
                            hook(g)

                items = [(h, b) for h in range(RH) for b in blocks]
                for n in range(len(items) + 2):
                    if n < len(items):
                        h, b = items[n]
                        j = b - blocks[0]
                        tl = open_tile(("r", h, b))
                        for half, kind in enumerate(("qk", "vg")):
                            w = weights(g, kind, h)
                            for c in range(DC):
                                ins = pe.matmul(tl.ap[:, half * CW:(half + 1) * CW], a_t[:, c, j * P:(j + 1) * P],
                                                w[:, c, :], start=c == 0, stop=c == DC - 1)
                            release(g, kind, h, tl)
                        ins.then_inc(tl.full[0], 1)
                    if 1 <= n <= len(items):
                        h, b = items[n - 1]
                        k = (n - 1) % 3
                        pe.wait_ge(ret_roped.sem, nth(h, b, RH))
                        tl = open_tile(("r_t", h, b))
                        turn_over(tl, lambda i: ret_qk[:, k, i * RD:(i + 1) * RD], 2)
                    if n >= 2:
                        h, b = items[n - 2]
                        k = (n - 2) % 3
                        pe.wait_ge(ret_s_ready.sem, nth(h, b, RH))
                        tl = open_tile(("r_o", h, b))
                        ins = pe.matmul(tl.ap[:, 0:RD], ret_s[:, k, :], ret_in[:, k, 2 * RD:3 * RD],
                                        start=True, stop=b == 0)
                        if b:
                            pe.wait_ge(r_ready.sem, r_count(h, b - 1))
                            ins = pe.matmul(tl.ap[:, 0:RD], ret_qk_t[:, k, 0:RD], r_state[:, h, :],
                                            start=False, stop=True)
                        ins.then_inc(tl.full[0], 1)
                        if b < NBLK - 1:
                            pe.wait_ge(ret_kz_ready.sem, nth(h, b, RH))
                            tl = open_tile(("r_kv", h, b))
                            pe.matmul(tl.ap[:, 0:RD], ret_kz[:, k, :], ret_in[:, k, 2 * RD:3 * RD],
                                      start=True, stop=True).then_inc(tl.full[0], 1)
                    if 1 <= n <= len(items):
                        h, b = items[n - 1]
                        k = (n - 1) % 3
                        pe.wait_ge(*tile("r_t", h, b).free)
                        tl = open_tile(("r_s", h, b))
                        pe.matmul(tl.ap[:, 0:P], ret_qk_t[:, k, RD:2 * RD], ret_qk_t[:, k, 0:RD],
                                  start=True, stop=True).then_inc(tl.full[0], 1)
                    if n < len(items):
                        hook(g)

                left_operand("out_t", blocks, mixed, lambda b: b + 1)
                for c in range(4):
                    rows_product(g, "o", c, CW, blocks, "wo", "out_t")
                    hook(g)

                left_operand("x_t", blocks, normed, lambda b: norm_no[("x", b)] + 1)
                items = [(h, b) for h in range(XH) for b in blocks]
                for n in range(len(items) + LAG):
                    if n < len(items):
                        h, b = items[n]
                        j = b - blocks[0]
                        if j == 0:
                            columns_product(g, "xq", h, blocks, ("xq", g), "x_t")
                            pe.wait_ge(*tile(("xq", g), h, 0).free)
                            pe.wait_ge(*tile(("xq", g), h, 1).free)
                        tl = open_tile(("xs", h, b))
                        for i in range(2):
                            ins = pe.matmul(tl.ap[:, 0:MEM], xq_t[:, h % 2, i, j * P:(j + 1) * P], xk[:, 2 * h + i, :],
                                            start=i == 0, stop=i == 1)
                        ins.then_inc(tl.full[0], 1)
                    if n >= LAG:
                        i = n - LAG
                        h, b = items[i]
                        pe.wait_ge(*tile("xs", h, b).free)
                        tl = open_tile(("xp_t", h, b))
                        turn_over(tl, lambda c: probs[:, i % (LAG + 1), c * P:(c + 1) * P], MT)
                        pe.wait_ge(*tl.free)
                        tl = open_tile(("xo", h, b))
                        for m in range(MT):
                            ins = pe.matmul(tl.ap[:, 0:XD], probs_t[:, i % 2, m * P:(m + 1) * P],
                                            xv[:, m, h * XD:(h + 1) * XD], start=m == 0, stop=m == MT - 1)
                        ins.then_inc(tl.full[0], 1)
                    if n < len(items):
                        hook(g)
                left_operand("xo_t", blocks, x_out, lambda b: nth(XH - 1, b, XH))
                for c in range(4):
                    rows_product(g, "xo", c, CW, blocks, "wxo", "xo_t")
                    hook(g)

                left_operand("f_t", blocks, normed, lambda b: norm_no[("ffn", b)] + 1)
                for h in range(PH + 1):
                    if h < PH:
                        columns_product(g, "pq", h, blocks, ("pq", g), "f_t")
                    if h >= 1:
                        for i in range(2):
                            pe.wait_ge(*tile(("pq", g), h - 1, i).free)
                        for j, b in enumerate(blocks):
                            tl = open_tile(("ps", h - 1, b))
                            for i in range(2):
                                ins = pe.matmul(tl.ap[:, i * KEYS:(i + 1) * KEYS],
                                                xq_t[:, (h - 1) % 2, i, j * P:(j + 1) * P], sk[:, i, :],
                                                start=True, stop=True)
                            ins.then_inc(tl.full[0], 1)
                            for _ in range(3):
                                hook(g)

            experts(later)
            for b in GROUPS[-1]:
                first, last = max(loop_from, b * PH), (b + 1) * PH - 1
                if first % PH == 0:
                    experts(range(first * HEAD_STEPS, (first + 1) * HEAD_STEPS))
                    first += 1

                def head_steps(head):
                    for step in range(HEAD_STEPS):
                        expert_step(head, step)

                in_loops(pe, first, last, head_steps)
                experts(range(last * HEAD_STEPS, (last + 1) * HEAD_STEPS))

        @block.sync
        def _(sp):
            def rows_of(gain):
                return gain.rearrange("(a n) -> a n", a=1)

            sp.dma_start(h_sb[:, 0, :], t["x"][0, 0:P, :]).then_inc(x_in[0], 16)
            sp.dma_start(cst[:, :], consts).then_inc(const_in, 16)

            def gain(name):
                n = list(GAINS).index(name)
                sp.dma_start(g_cols[:, n, 0:GAINS[name]], t[name][0].rearrange("(c p) -> p c", p=P),
                             allow_slow_non_contiguous=True).then_inc(gains_in, 16)

            gain("g_mix")

            def load_chunk(no):
                g, kind, n = chunks[no]
                slot = no % W_SLOTS
                if no >= W_SLOTS:
                    sp.wait_ge(*chunk_freed[chunks[no - W_SLOTS]])
                dst = w_ring[:, slot, :].rearrange("p (c n) -> p c n", c=DC)
                if kind == "uq":
                    w = t["w_uq"][0].rearrange("(c p) n -> p c n", p=P)
                    dst = w_ring[:, slot, 0:3 * 384].rearrange("p (c n) -> p c n", c=3)
                    parts = [(dst[:, 0:1, :], w[:, 0:1, n * 384:(n + 1) * 384]),
                             (dst[:, 1:3, :], w[:, 1:3, n * 384:(n + 1) * 384])]
                elif kind == "ukv":
                    w = t["w_ukv"][0].rearrange("(c p) n -> p c n", p=P)
                    dst = w_ring[:, slot, :].rearrange("p (c n) -> p c n", c=2)
                    parts = [(dst[:, i, :], w[:, i, :]) for i in range(2)]
                elif kind in ("qk", "vg"):
                    w = t["w_in"][0].rearrange("(c p) n -> p c n", p=P)
                    first = QR + KVR + ROPE + (0 if kind == "qk" else 2 * RH * RD) + n * RD
                    parts = [(dst[:, :, i * RD:(i + 1) * RD],
                              w[:, :, first + i * RH * RD:first + i * RH * RD + RD]) for i in range(2)]
                else:
                    name, first, width = {
                        "in": ("w_in", n * CW, min(CW, QR + KVR + ROPE - n * CW)),
                        "o": ("w_o", n * CW, CW), "xk": ("w_xkv", n * CW, CW),
                        "xv": ("w_xkv", D + n * CW, CW), "xq": ("w_xq", n * CW, CW),
                        "xo": ("w_xo", n * CW, CW), "pq": ("w_pq", n * CW, CW)}[kind]
                    w = t[name][0].rearrange("(c p) n -> p c n", p=P)
                    parts = [(dst[:, i:i + 4, 0:width], w[:, i:i + 4, first:first + width]) for i in (0, 4)]
                for d, s in parts:
                    sp.dma_start(d, s).then_inc(w_in_slot[slot], 16)

            for no in range(W_SLOTS):
                load_chunk(no)
            for m in range(MT):
                sp.dma_start(mem_rows[:, m, :], t["mem"][0, m * P:(m + 1) * P, :]).then_inc(mem_in, 16)
            sp.dma_start(rows[:, 1, 0:2 * P].rearrange("k (p d) -> k p d", p=2),
                         t["sub_keys"][0].rearrange("p k d -> k p d")).then_inc(sub_in, 16)
            for name in list(GAINS)[1:]:
                gain(name)
            sp.dma_start(g_rows[:, :], t["g_ffn"][0].partition_broadcast(P)).then_inc(g_rows_in, 16)
            for b in range(1, NBLK):
                sp.dma_start(h_sb[:, b, :], t["x"][0, b * P:(b + 1) * P, :]).then_inc(x_in[b], 16)
            for no in range(W_SLOTS, len(chunks)):
                load_chunk(no)
            sp.wait_ge(t_ready.sem, NBLK)
            sp.dma_start(g_rows[:, :], t["g_final"].partition_broadcast(P)).then_inc(g_rows_in, 16)
            for b in range(NBLK):
                sp.wait_ge(out_ready.sem, b + 1)
                sp.dma_start(out[0, b * P:(b + 1) * P, :], rows[:, b, :]).then_inc(out_done, 16)
            sp.wait_ge(out_done, 16 * NBLK)

        @block.scalar
        def _(act):
            def link(ins, sig=act_step):
                ins.then_inc(sig.sem, 1)
                sig.n += 1
                act.wait_ge(sig.sem, sig.n)

            def empty(tl, dst, src):
                nc.scalar.activation(dst, src, ACT.Copy).then_inc(tl.free[0], 1)
                act.wait_ge(*tl.free)

            def square_root(kind, b, src, junk):
                n = norm_no[(kind, b)]
                link(nc.scalar.activation(junk, src, ACT.Square, accum_out=ssq[:, n:n + 1]))
                link(nc.scalar.activation(std[:, n:n + 1], ssq[:, n:n + 1], ACT.Sqrt, bias=eps, scale=1.0 / D),
                     std_ready)

            def empty_scaled(tl, dst, n, gain, first):
                g_no = list(GAINS).index(gain)
                for c in range(n):
                    ins = nc.scalar.activation(dst[:, c, :], tl.ap[:, c * P:(c + 1) * P], ACT.Copy,
                                               scale=g_cols[:, g_no, first + c:first + c + 1])
                    if c < n - 1:
                        ins.then_inc(act_step.sem, 1)
                        act_step.n += 1
                ins.then_inc(tl.free[0], 1)
                act.wait_ge(*tl.free)

            def left_operand(kind, blocks, gain=None):
                for j, b in enumerate(blocks):
                    for i in range(2):
                        tl = tile(kind, b, i)
                        act.wait_ge(*tl.full)
                        dst = a_t[:, 4 * i:4 * i + 4, j * P:(j + 1) * P]
                        if gain is None or (gain == "g_ret_gn" and i == 0):
                            empty(tl, dst, tl.ap[:, :].rearrange("p (c n) -> p c n", c=4))
                        else:
                            empty_scaled(tl, dst, 4, gain, 0 if gain == "g_ret_gn" else 4 * i)

            def expert_step(head, step):
                k = step - TOPK - 1
                if step == TOPK:
                    act.wait_ge(dve_used, head.times(DVE_ROWS, DVE_ROWS + TOPK))
                    nc.scalar.activation(acts[:, :], dots[:, :], ACT.Gelu).then_inc(gelu_ready, 1)
                    act.wait_ge(gelu_ready, head.times(1, 1))
                    act.wait_ge(weights_ready, head.times(1, 1))
                elif k >= 0 and k % 2 == 1:
                    act.wait_ge(pe_used, head.times(PE_ROWS, k // 2 + 1))
                    nc.scalar.activation(diag[:, k // 2, :], ident, ACT.Copy, scale=pick_w[:, k:k + 1])\
                        .then_inc(diag_ready, 1)

            place = [0]

            def hook(g):
                for at_step in plan[(g, place[0])]:
                    n, step = divmod(at_step, HEAD_STEPS)
                    expert_step(Head(n), step)
                place[0] = place[0] + 1 if (g, place[0] + 1) in plan else 0

            act.wait_ge(const_in, 16)
            for g, blocks in enumerate(GROUPS):
                nb = len(blocks)
                for j, b in enumerate(blocks):
                    act.wait_ge(x_in[b], 16)
                    if g:
                        act.wait_ge(*tile("f_t", GROUPS[g - 1][-1], 1).full)
                    square_root("mix", b, h_sb[:, b, :], mix[:, j, :])
                if g == 0:
                    act.wait_ge(mem_in, 16 * MT)
                    for m in range(MT):
                        square_root("mem", m, mem_rows[:, m, :], rows[:, 0, :])
                    act.wait_ge(*tile("sk").full)
                    empty(tile("sk"), sk[:, :, :], tile("sk").ap[:, 0:2 * P].rearrange("p (c n) -> p c n", c=2))
                if g == 0:
                    act.wait_ge(gains_in, 16 * len(GAINS))
                left_operand("mix_t", blocks, "g_mix")
                if g:
                    act.wait_ge(expert_ready.sem, nth(PH - 1, GROUPS[g - 1][-1], PH))
                for c in range(3):
                    for j, b in enumerate(blocks):
                        tl = tile("mp", c, b)
                        w = min(CW, QR + KVR + ROPE - c * CW)
                        act.wait_ge(*tl.full)
                        empty(tl, mp[:, j, c * CW:c * CW + w], tl.ap[:, 0:w])

                if g == 0:
                    for m in range(MT):
                        for i in range(2):
                            tl = tile("mem_t", m, i)
                            act.wait_ge(*tl.full)
                            empty_scaled(tl, mem_t[:, 4 * i:4 * i + 4, m * P:(m + 1) * P], 4, "g_mem", 4 * i)

                for j, b in enumerate(blocks):
                    if b:
                        act.wait_ge(q_roped.sem, b)
                    link(nc.scalar.activation(probs[:, 0, 0:QR], mp[:, j, 0:QR], ACT.Square,
                                              accum_out=lora[:, 0, 0:1]))
                    link(nc.scalar.activation(probs[:, 0, 0:KVR], mp[:, j, QR:QR + KVR], ACT.Square,
                                              accum_out=lora[:, 1, 0:1]))
                    link(nc.scalar.activation(lora[:, 0, 1:2], lora[:, 0, 0:1], ACT.Sqrt, bias=eps, scale=1.0 / QR))
                    link(nc.scalar.activation(lora[:, 1, 1:2], lora[:, 1, 0:1], ACT.Sqrt, bias=eps, scale=1.0 / KVR),
                         lora_std)
                    for i, n in ((0, 3), (1, 2)):
                        tl = tile("lora_t", b, i)
                        act.wait_ge(*tl.full)
                        empty_scaled(tl, lora_t[:, 3 * i:3 * i + n, :], n, "g_kv_lora" if i else "g_q_lora", 0)
                    for i in range(2):
                        tl = tile("q", b, i)
                        act.wait_ge(*tl.full)
                        empty(tl, q_cat[:, 4 * i:4 * i + 4, :], tl.ap[:, 0:4 * QK].rearrange("p (c n) -> p c n", c=4))
                    for i in range(2):
                        tl = tile("kv", b, i)
                        kv = tl.ap[:, :].rearrange("p (c n) -> p c n", c=4)
                        act.wait_ge(*tl.full)
                        link(nc.scalar.activation(k_cat[:, 4 * i:4 * i + 4, 0:NOPE], kv[:, :, 0:NOPE], ACT.Copy))
                        empty(tl, v_mla[:, b, 4 * i:4 * i + 4, :], kv[:, :, NOPE:NOPE + VD])
                    for i in range(2):
                        tl = tile("k_t", b, i)
                        act.wait_ge(*tl.full)
                        empty(tl, k_mla[:, 4 * i:4 * i + 4, b * P:(b + 1) * P],
                              tl.ap[0:QK, :].rearrange("p (c n) -> p c n", c=4))
                    for i in range(2):
                        tl = tile("q_t", b, i)
                        act.wait_ge(*tl.full)
                        empty(tl, q_t[0:QK, 4 * i:4 * i + 4, :], tl.ap[0:QK, :].rearrange("p (c n) -> p c n", c=4))
                    if b:
                        act.wait_ge(mla_out.sem, b)
                    for h in range(H + LAG):
                        if h < H:
                            tl = tile("s", b, h)
                            act.wait_ge(mla_top.sem, b * H + h + 1)
                            nc.scalar.activation(probs[:, h % (LAG + 1), 0:(b + 1) * P], tl.ap[:, 0:(b + 1) * P],
                                                 ACT.Exp, bias=top[:, h % (LAG + 1):h % (LAG + 1) + 1],
                                                 scale=MLA_SCALE, accum_out=den[:, h:h + 1]).then_inc(tl.free[0], 1)
                            act.wait_ge(*tl.free)
                        if h >= LAG:
                            i = h - LAG
                            tl = tile("p_t", b, i)
                            act.wait_ge(*tl.full)
                            empty(tl, probs_t[:, i % 2, 0:(b + 1) * P], tl.ap[:, 0:(b + 1) * P])
                        if g == 0 and h < 2 * XH:
                            for i in range(2):
                                tl = tile("xk" if h % 2 == 0 else "xv", h // 2, i)
                                act.wait_ge(*tl.full)
                                if h % 2 == 0:
                                    empty(tl, xk[:, h + i, :], tl.ap[:, 0:MEM])
                                else:
                                    empty(tl, xv[:, i, h // 2 * XD:(h // 2 + 1) * XD], tl.ap[:, 0:XD])
                        if h < H:
                            hook(g)

                act.wait_ge(mla_out.sem, blocks[-1] + 1)
                items = [(h, b) for h in range(RH) for b in blocks]
                for n in range(len(items) + 1):
                    if n < len(items):
                        h, b = items[n]
                        k = n % 3
                        tl = tile("r", h, b)
                        act.wait_ge(*tl.full)
                        if n >= 3:
                            act.wait_ge(ret_gated.sem, nth(*items[n - 3], RH))
                        empty(tl, ret_in[:, k, :], tl.ap[:, :])
                        if n >= 1:
                            act.wait_ge(ret_gated.sem, nth(*items[n - 1], RH))
                        link(nc.scalar.activation(ret_e, ret_in[:, k, 3 * RD:], ACT.Exp, scale=-1.0), ret_exp)
                    if n >= 1:
                        h, b = items[n - 1]
                        k = (n - 1) % 3
                        act.wait_ge(ret_roped.sem, nth(h, b, RH))
                        z = CONST["zeta"][0] + h
                        link(nc.scalar.activation(ret_kz[:, k, :], ret_qk[:, k, RD:], ACT.Copy,
                                                  scale=cst[:, z:z + 1]), ret_kz_ready)
                        tl = tile("r_t", h, b)
                        act.wait_ge(*tl.full)
                        empty(tl, ret_qk_t[:, k, :], tl.ap[:, 0:2 * RD])
                    if n < len(items):
                        hook(g)
                for j, b in enumerate(blocks):
                    act.wait_ge(gn_var.sem, b + 1)
                    link(nc.scalar.activation(gn_s[:, 1, :], gn_s[:, 0, :], ACT.Sqrt, bias=eps), gn_std)

                left_operand("out_t", blocks, "g_ret_gn")
                for c in range(4):
                    hook(g)
                for j, b in enumerate(blocks):
                    act.wait_ge(mix_added.sem, nth(3, b, 4))
                    act.wait_ge(*tile("out_t", b, 1).full)
                    square_root("x", b, h_sb[:, b, :], mix[:, j, :])
                left_operand("x_t", blocks, "g_xattn")
                items = [(h, b) for h in range(XH) for b in blocks]
                for n in range(len(items) + LAG):
                    if n < len(items):
                        h, b = items[n]
                        if b == blocks[0]:
                            for i in range(2):
                                tl = tile(("xq", g), h, i)
                                act.wait_ge(*tl.full)
                                empty(tl, xq_t[:, h % 2, i, 0:nb * P], tl.ap[:, 0:nb * P])
                        tl = tile("xs", h, b)
                        k = n % (LAG + 1)
                        act.wait_ge(x_top.sem, nth(h, b, XH))
                        nc.scalar.activation(probs[:, k, 0:MEM], tl.ap[:, 0:MEM], ACT.Exp, bias=top[:, k:k + 1],
                                             scale=X_SCALE, accum_out=den[:, k:k + 1]).then_inc(tl.free[0], 1)
                        act.wait_ge(*tl.free)
                    if n >= LAG:
                        h, b = items[n - LAG]
                        tl = tile("xp_t", h, b)
                        act.wait_ge(*tl.full)
                        empty(tl, probs_t[:, (n - LAG) % 2, 0:MEM], tl.ap[:, 0:MEM])
                        act.wait_ge(x_out.sem, nth(h, b, XH))
                    if n < len(items):
                        hook(g)
                left_operand("xo_t", blocks)
                for c in range(4):
                    hook(g)
                for j, b in enumerate(blocks):
                    act.wait_ge(x_added.sem, nth(3, b, 4))
                    act.wait_ge(*tile("xo_t", b, 1).full)
                    square_root("ffn", b, h_sb[:, b, :], mix[:, j, :])

                left_operand("f_t", blocks, "g_ffn")
                for h in range(PH + 1):
                    if h < PH:
                        for i in range(2):
                            tl = tile(("pq", g), h, i)
                            act.wait_ge(*tl.full)
                            empty(tl, xq_t[:, h % 2, i, 0:nb * P], tl.ap[:, 0:nb * P])
                    if h >= 1:
                        for b in blocks:
                            hook(g)
                            act.wait_ge(best_ready.sem, nth(h - 1, b, PH))
                            link(nc.scalar.activation(soft, best, ACT.Exp, bias=small[:, 0:1],
                                                      accum_out=small[:, 1:2]), soft_ready)
                            hook(g)
                            hook(g)

            def head_steps(head):
                for step in range(HEAD_STEPS):
                    expert_step(head, step)

            in_loops(act, loop_from, NBLK * PH, head_steps)
            for b in range(NBLK):
                act.wait_ge(sum_taken.sem, b + 1)
                square_root("fin", b, h_sb[:, b, :], mix[:, 0, :])

        @block.vector
        def _(dve):
            def link(ins, sig=dve_step, hold=True):
                ins.then_inc(sig.sem, 1)
                sig.n += 1
                if hold:
                    dve.wait_ge(sig.sem, sig.n)

            def last_read(ins, tl):
                ins.then_inc(tl.free[0], 1)
                dve.wait_ge(*tl.free)

            def spread(ap, *shape):
                return ap.to_broadcast([P, *shape])

            def norm(kind, b, src, dst, gain=None):
                n = norm_no[(kind, b)]
                dve.wait_ge(std_ready.sem, n + 1)
                link(nc.vector.reciprocal(rstd[:, n:n + 1], std[:, n:n + 1]))
                if gain is None:
                    ins = nc.vector.tensor_scalar(dst, src, rstd[:, n:n + 1], None, ALU.mult)
                else:
                    ins = nc.vector.scalar_tensor_tensor(dst, src, rstd[:, n:n + 1], gain, ALU.mult, ALU.mult)
                ins.then_inc(normed.sem, 1)
                dve.wait_ge(normed.sem, n + 1)

            def rotate(x, dst, cos, sin, n, half, sig):
                a = rot_a[:, 0:n * 2 * half].rearrange("p (n t f) -> p n t f", n=n, t=2)
                b = rot_b[:, 0:n * 2 * half].rearrange("p (n t f) -> p n t f", n=n, t=2)
                c4 = cos.unsqueeze(1).unsqueeze(1).to_broadcast([P, n, 2, half])
                s4 = sin.unsqueeze(1).unsqueeze(1).to_broadcast([P, n, 2, half])
                link(nc.vector.tensor_tensor(a, x, c4, ALU.mult), hold=False)
                link(nc.vector.tensor_tensor(b, x, s4, ALU.mult))
                link(nc.vector.tensor_tensor(dst[:, :, 0, :], a[:, :, 0, :], b[:, :, 1, :], ALU.subtract))
                link(nc.vector.tensor_tensor(dst[:, :, 1, :], b[:, :, 0, :], a[:, :, 1, :], ALU.add), sig)

            def add_product(g, tag, blocks, sig):
                for c in range(4):
                    for b in blocks:
                        tl = tile(tag, c, b)
                        dve.wait_ge(*tl.full)
                        hb = h_sb[:, b, c * CW:(c + 1) * CW]
                        last_read(nc.vector.tensor_tensor(hb, hb, tl.ap[:, 0:CW], ALU.add), tl)
                        dve.sem_inc(sig.sem, 1)
                        sig.n += 1
                    hook(g)

            def expert_step(head, b, step):
                if step < TOPK:
                    s = head.slot(step)
                    dve.wait_ge(row_in[s], head.landed(step))
                    nc.vector.tensor_tensor_reduce(out=rows[:, s, :], in0=rows[:, s, :], in1=t_cur[:, :], scale=1.0,
                                                   scalar=0.0, op0=ALU.mult, op1=ALU.add,
                                                   accum_out=dots[:, step:step + 1]).then_inc(dve_used, 1)
                elif step == TOPK:
                    dve.wait_ge(gelu_ready, head.times(1, 1))
                    if not (isinstance(head.turn, int) and head.at == 0):
                        dve.wait_ge(diag_ready, head.times(PE_ROWS, 0))
                    if isinstance(head.turn, int):
                        g_n = gate[:, head.at, :]
                    else:
                        g_n = gate[:, bass.ds(head.times(1, 0), 1), :].rearrange("p a k -> p (a k)")
                    nc.vector.tensor_tensor(pick_w[:, :], acts[:, :], g_n, ALU.mult).then_inc(weights_ready, 1)
                    dve.wait_ge(weights_ready, head.times(1, 1))
                elif (step - TOPK - 1) % 2 == 0:
                    k = step - TOPK - 1
                    s = head.slot(TOPK + k)
                    dve.wait_ge(row_in[s], head.landed(TOPK + k))
                    nc.vector.scalar_tensor_tensor(h_sb[:, b, :], rows[:, s, :], pick_w[:, k:k + 1], h_sb[:, b, :],
                                                   ALU.mult, ALU.add).then_inc(dve_used, 1)
                    dve.wait_ge(dve_used, head.times(DVE_ROWS, DVE_ROWS + TOPK + k // 2 + 1))

            place = [0]

            def hook(g):
                for at_step in plan[(g, place[0])]:
                    n, step = divmod(at_step, HEAD_STEPS)
                    if step == 0 and n % PH == 0:
                        expert_tokens(n // PH)
                    expert_step(Head(n), n // PH, step)
                place[0] = place[0] + 1 if (g, place[0] + 1) in plan else 0

            def take_sum(b):
                dve.wait_ge(pe_used, PE_ROWS + (b + 1) * PH * PE_ROWS)
                for i in range(2):
                    hb = h_sb[:, b, i * 512:(i + 1) * 512]
                    link(nc.vector.tensor_tensor(hb, hb, banks[SUM_BANK + i][:, :], ALU.add),
                         sum_taken if i else dve_step)

            def expert_tokens(b):
                if b:
                    take_sum(b - 1)
                else:
                    dve.wait_ge(g_rows_in, 16)
                n = norm_no[("ffn", b)]
                link(nc.vector.scalar_tensor_tensor(t_cur[:, :], h_sb[:, b, :], rstd[:, n:n + 1], g_rows[:, :],
                                                    ALU.mult, ALU.mult), t_ready)

            def choose(g, h, b):
                tl = tile("ps", h, b)
                dve.wait_ge(*tl.full)
                scores = [tl.ap[:, p * KEYS:(p + 1) * KEYS] for p in range(2)]
                for p in range(2):
                    link(nc.vector.max(key_s[:, p, 0:8], scores[p]), hold=p == 1)
                for p in range(2):
                    link(nc.vector.match_replace(rest[:, p, :], key_s[:, p, 0:8], scores[p], LOW), hold=p == 1)
                for p in range(2):
                    link(nc.vector.max(key_s[:, p, 8:16], rest[:, p, :]), hold=p == 1)
                for p in range(2):
                    link(nc.vector.max_index(key_i[:, p, 8:16], key_s[:, p, 8:16], rest[:, p, :]), hold=False)
                link(nc.vector.max_index(key_i[:, 0, 0:8], key_s[:, 0, 0:8], scores[0]), hold=False)
                last_read(nc.vector.max_index(key_i[:, 1, 0:8], key_s[:, 1, 0:8], scores[1]), tl)
                hook(g)
                link(nc.vector.tensor_tensor(cand, key_s[:, 0, :].unsqueeze(2).to_broadcast([P, TOPK, TOPK]),
                                             key_s[:, 1, :].unsqueeze(1).to_broadcast([P, TOPK, TOPK]), ALU.add))
                pairs = cand.rearrange("p a b -> p (a b)")
                link(nc.vector.max(best[:, 0:8], pairs))
                link(nc.vector.match_replace(cand2, best[:, 0:8], pairs, LOW))
                link(nc.vector.max(best[:, 8:16], cand2))
                link(nc.vector.tensor_scalar(small[:, 0:1], best[:, 0:1], -1.0, None, ALU.mult), best_ready,
                     hold=False)
                link(nc.vector.max_index(best_c[:, 0:8], best[:, 0:8], pairs), hold=False)
                link(nc.vector.max_index(best_c[:, 8:16], best[:, 8:16], cand2), hold=True)
                hook(g)
                link(nc.vector.tensor_scalar(split[:, 0, :], best_c[:, :], 4, None, ALU.logical_shift_right),
                     hold=False)
                link(nc.vector.tensor_scalar(split[:, 1, :], best_c[:, :], 15, None, ALU.bitwise_and))
                for p in range(2):
                    link(nc.vector.tensor_tensor(hit[:, p, :, :],
                                                 split[:, p, :].unsqueeze(2).to_broadcast([P, TOPK, TOPK]),
                                                 const("iota").unsqueeze(1).to_broadcast([P, TOPK, TOPK]),
                                                 ALU.is_equal), hold=p == 1)
                for p in range(2):
                    link(nc.vector.tensor_tensor(hit2[:, p, :, :], hit[:, p, :, :],
                                                 key_i[:, p, :].unsqueeze(1).to_broadcast([P, TOPK, TOPK]),
                                                 ALU.mult), hold=p == 1)
                link(nc.vector.tensor_reduce(picked, hit2, AX.X, ALU.add))
                dve.wait_ge(soft_ready.sem, nth(h, b, PH))
                link(nc.vector.reciprocal(small[:, 2:3], small[:, 1:2]))
                link(nc.vector.tensor_scalar(gate[:, b * PH + h, :], soft, small[:, 2:3], None, ALU.mult))
                link(nc.vector.scalar_tensor_tensor(expert[:, b * PH + h, :], picked[:, 0, :], float(KEYS),
                                                    picked[:, 1, :], ALU.mult, ALU.add), expert_ready)

            dve.sem_inc(dve_used, DVE_ROWS)
            dve.sem_inc(pe_used, PE_ROWS)
            dve.wait_ge(const_in, 16)
            for g, blocks in enumerate(GROUPS):
                nb = len(blocks)
                for j, b in enumerate(blocks):
                    norm("mix", b, h_sb[:, b, :], mix[:, j, :])
                if g == 0:
                    for m in range(MT):
                        norm("mem", m, mem_rows[:, m, :], mem_rows[:, m, :])

                for j, b in enumerate(blocks):
                    dve.wait_ge(lora_std.sem, b + 1)
                    link(nc.vector.reciprocal(lora[:, :, 2], lora[:, :, 1]))
                    qv, kv = mp[:, j, 0:QR], mp[:, j, QR:QR + KVR]
                    link(nc.vector.tensor_scalar(qv, qv, lora[:, 0, 2:3], None, ALU.mult), hold=False)
                    link(nc.vector.tensor_scalar(kv, kv, lora[:, 1, 2:3], None, ALU.mult), lora_normed)
                    cos = const("mla_cos")[:, b * 16:(b + 1) * 16]
                    sin = const("mla_sin")[:, b * 16:(b + 1) * 16]
                    rotate(mp[:, j, QR + KVR:].rearrange("p (n t f) -> p n t f", n=1, t=2),
                           kpe[:, :].rearrange("p (n t f) -> p n t f", n=1, t=2), cos, sin, 1, 16, dve_step)
                    dve.wait_ge(*tile("kv", b, 1).free)
                    link(nc.vector.tensor_copy(k_cat[:, :, NOPE:],
                                               kpe[:, :].unsqueeze(1).to_broadcast([P, H, ROPE])), k_joined)
                    qr = q_cat[:, :, NOPE:].rearrange("p n (t f) -> p n t f", t=2)
                    rotate(qr, qr, cos, sin, H, 16, q_roped)
                    for h in range(H):
                        tl = tile("s", b, h)
                        k = h % (LAG + 1)
                        dve.wait_ge(*tl.full)
                        diag = tl.ap[:, b * P:(b + 1) * P]
                        link(nc.vector.tensor_tensor(diag, diag, const("causal"), ALU.add))
                        link(nc.vector.tensor_reduce(mx[:, :], tl.ap[:, 0:(b + 1) * P], AX.X, ALU.max))
                        if h > LAG:
                            dve.wait_ge(*tile("s", b, h - LAG - 1).free)
                        link(nc.vector.tensor_scalar(top[:, k:k + 1], mx[:, :], -MLA_SCALE, None, ALU.mult), mla_top)
                        hook(g)
                    to = tile("o", b)
                    dve.wait_ge(*to.full)
                    link(nc.vector.reciprocal(rden[:, :], den[:, :]))
                    last_read(nc.vector.tensor_tensor(
                        mix[:, j, 0:H * VD].rearrange("p (h d) -> p h d", h=H),
                        to.ap[:, :].rearrange("p (h d) -> p h d", h=H),
                        rden[:, :].unsqueeze(2).to_broadcast([P, H, VD]), ALU.mult), to)
                    dve.sem_inc(mla_out.sem, 1)
                    mla_out.n += 1

                items = [(h, b) for h in range(RH) for b in blocks]
                for n in range(len(items) + 2):
                    if n < len(items):
                        h, b = items[n]
                        k = n % 3
                        dve.wait_ge(*tile("r", h, b).free)
                        rotate(ret_in[:, k, 0:2 * RD].rearrange("p (n t f) -> p n t f", n=2, t=2),
                               ret_qk[:, k, :].rearrange("p (n t f) -> p n t f", n=2, t=2),
                               const("ret_cos")[:, b * 64:(b + 1) * 64], const("ret_sin")[:, b * 64:(b + 1) * 64],
                               2, 64, ret_roped)
                        dve.wait_ge(ret_exp.sem, nth(h, b, RH))
                        link(nc.vector.tensor_scalar(ret_sig, ret_e, 1.0, None, ALU.add))
                        link(nc.vector.reciprocal(ret_sig, ret_sig))
                        link(nc.vector.tensor_tensor(ret_gate[:, k, :], ret_sig, ret_in[:, k, 3 * RD:], ALU.mult),
                             ret_gated)
                        hook(g)
                    if n >= 2:
                        h, b = items[n - 2]
                        k = (n - 2) % 3
                        j = b - blocks[0]
                        tl = tile("r_o", h, b)
                        dve.wait_ge(*tl.full)
                        link(nc.vector.bn_stats(gn_stats[:, :], tl.ap[:, 0:RD]))
                        link(nc.vector.bn_aggr(gn[:, j, h, :], gn_stats[:, :]))
                        last_read(nc.vector.scalar_tensor_tensor(
                            mix[:, j, H * VD + h * RD:H * VD + (h + 1) * RD], tl.ap[:, 0:RD], gn[:, j, h, 0:1],
                            ret_gate[:, k, :], ALU.subtract, ALU.mult), tl)
                        if b < NBLK - 1:
                            tl = tile("r_kv", h, b)
                            dve.wait_ge(*tl.full)
                            if b == 0:
                                ins = nc.vector.tensor_copy(r_state[:, h, :], tl.ap[:, 0:RD])
                            else:
                                ins = nc.vector.scalar_tensor_tensor(
                                    r_state[:, h, :], r_state[:, h, :], float((1.0 - 2.0 ** (-5.0 - h)) ** P),
                                    tl.ap[:, 0:RD], ALU.mult, ALU.add)
                            last_read(ins, tl)
                            dve.sem_inc(r_ready.sem, 1)
                            r_ready.n += 1
                    if 1 <= n <= len(items):
                        h, b = items[n - 1]
                        k = (n - 1) % 3
                        tl = tile("r_s", h, b)
                        dve.wait_ge(*tl.full)
                        z = CONST["key_decay"][0] + h
                        last_read(nc.vector.scalar_tensor_tensor(ret_s[:, k, :], tl.ap[:, 0:P], cst[:, z:z + 1],
                                                                 const("ret_mask"), ALU.mult, ALU.mult), tl)
                        dve.sem_inc(ret_s_ready.sem, 1)
                        ret_s_ready.n += 1
                for j, b in enumerate(blocks):
                    link(nc.vector.tensor_tensor(gn_s[:, 0, :], gn[:, j, :, 1], const("xi2"), ALU.mult), gn_var)
                    dve.wait_ge(gn_std.sem, b + 1)
                    link(nc.vector.reciprocal(gn_s[:, 2, :], gn_s[:, 1, :]))
                    link(nc.vector.tensor_tensor(gn_s[:, 3, :], gn_s[:, 2, :], const("xi"), ALU.mult))
                    o = mix[:, j, H * VD:].rearrange("p (h d) -> p h d", h=RH)
                    link(nc.vector.tensor_tensor(o, o, gn_s[:, 3, :].unsqueeze(2).to_broadcast([P, RH, RD]),
                                                 ALU.mult), mixed)
                add_product(g, "wo", blocks, mix_added)

                for j, b in enumerate(blocks):
                    norm("x", b, h_sb[:, b, :], mix[:, j, :])
                for j, b in enumerate(blocks):
                    dve.wait_ge(*tile("x_t", b, 1).full)
                items = [(h, b) for h in range(XH) for b in blocks]
                for n in range(len(items) + LAG):
                    if n < len(items):
                        h, b = items[n]
                        k = n % (LAG + 1)
                        tl = tile("xs", h, b)
                        dve.wait_ge(*tl.full)
                        link(nc.vector.tensor_reduce(mx[:, :], tl.ap[:, 0:MEM], AX.X, ALU.max))
                        link(nc.vector.tensor_scalar(top[:, k:k + 1], mx[:, :], -X_SCALE, None, ALU.mult), x_top)
                    if n >= LAG:
                        h, b = items[n - LAG]
                        k = (n - LAG) % (LAG + 1)
                        j = b - blocks[0]
                        tl = tile("xo", h, b)
                        dve.wait_ge(*tl.full)
                        link(nc.vector.reciprocal(rden[:, k:k + 1], den[:, k:k + 1]))
                        last_read(nc.vector.tensor_scalar(mix[:, j, h * XD:(h + 1) * XD], tl.ap[:, 0:XD],
                                                          rden[:, k:k + 1], None, ALU.mult), tl)
                        dve.sem_inc(x_out.sem, 1)
                        x_out.n += 1
                    if n < len(items):
                        hook(g)
                add_product(g, "wxo", blocks, x_added)

                for j, b in enumerate(blocks):
                    norm("ffn", b, h_sb[:, b, :], mix[:, j, :])
                for h in range(PH):
                    for b in blocks:
                        choose(g, h, b)
                        hook(g)

            for b in GROUPS[-1]:
                if b * PH >= loop_from:
                    expert_tokens(b)

                def head_steps(head):
                    for step in range(HEAD_STEPS):
                        expert_step(head, b, step)

                in_loops(dve, max(loop_from, b * PH), (b + 1) * PH, head_steps)
            take_sum(NBLK - 1)
            dve.wait_ge(g_rows_in, 32)
            for b in range(NBLK):
                norm("fin", b, h_sb[:, b, :], rows[:, b, :], g_rows[:, :])
                dve.sem_inc(out_ready.sem, 1)

        @block.gpsimd
        def _(pool):
            def slot_free(head, row):
                at, old = divmod(head.at * 2 * TOPK + row - ROWS, 2 * TOPK)
                before = Head(at, head.turn)
                if old < TOPK:
                    pool.wait_ge(dve_used, before.times(DVE_ROWS, DVE_ROWS + old + 1))
                elif old % 2 == 0:
                    pool.wait_ge(dve_used, before.times(DVE_ROWS, DVE_ROWS + TOPK + (old - TOPK) // 2 + 1))
                else:
                    pool.wait_ge(pe_used, before.times(PE_ROWS, PE_ROWS + (old - TOPK) // 2 + 1))

            def gathers(head):
                if isinstance(head.turn, int):
                    picks = expert[:, head.at, :]
                else:
                    picks = expert[:, bass.ds(head.times(1, 0), 1), :].rearrange("p a k -> p (a k)")
                for kind, (stage, table) in enumerate(((stage_u, t["u_experts"]), (stage_v, t["v_experts"]))):
                    nc.gpsimd.tensor_copy(stage[:, :], picks).then_inc(stage_step, 1)
                    pool.wait_ge(stage_step, head.times(2, kind + 1))
                    for k in range(TOPK):
                        row = kind * TOPK + k
                        s = head.slot(row)
                        slot_free(head, row)
                        pool.sem_inc(row_claimed, 1)
                        nc.gpsimd.indirect_dma_start(
                            rows[:, s, :], None, table[0],
                            bass.IndirectOffsetOnAxis(ap=stage[:, k:k + 1], axis=0)).then_inc(row_in[s], 16)

            for blocks in GROUPS:
                for j, b in enumerate(blocks):

                    def chosen_gathers(head):
                        nb = len(blocks)
                        pool.wait_ge(expert_ready.sem, head.times(nb, blocks[0] * PH + j + 1 - b * PH * nb))
                        gathers(head)

                    in_loops(pool, b * PH, (b + 1) * PH, chosen_gathers)


def r_count(h, b):
    n = 0
    for blocks in GROUPS:
        for hh in range(RH):
            for bb in blocks:
                if bb < NBLK - 1:
                    n += 1
                    if (hh, bb) == (h, b):
                        return n
    raise ValueError


_INS = ["x", "mem", "g_mix", "w_in", "g_q_lora", "w_uq", "g_kv_lora", "w_ukv", "g_ret_gn", "w_o", "g_xattn", "g_mem",
        "w_xq", "w_xkv", "w_xo", "g_ffn", "w_pq", "sub_keys", "u_experts", "v_experts", "g_final"]


def kernel(**inputs):
    import concourse.bacc as bacc
    from concourse.bass_utils import run_bass_kernel_spmd

    nc = bacc.Bacc("TRN2", target_bir_lowering=False, num_devices=1)
    arrays, t = {}, {}
    for name in _INS:
        a = np.ascontiguousarray(inputs[name])
        arrays[f"in_{name}"] = a
        t[name] = nc.dram_tensor(f"in_{name}", a.shape, mybir.dt.from_np(a.dtype), kind="ExternalInput").ap()
    arrays["in_consts"] = constants()
    consts = nc.dram_tensor("in_consts", (P, CONST_W), F32, kind="ExternalInput").ap()
    out = nc.dram_tensor("out_0", (1, SEQ, D), F32, kind="ExternalOutput").ap()
    build_trunk(nc, t, out, consts)
    r = run_bass_kernel_spmd(nc, [arrays], core_ids=[0])
    return r.results[0]["out_0"]
```

```python
from contextlib import ExitStack

import numpy as np

import concourse.bass as bass
from concourse import mybir

P = 128
ALU = mybir.AluOpType
ACT = mybir.ActivationFunctionType
AX = mybir.AxisListType
F32 = mybir.dt.float32
U32 = mybir.dt.uint32

SEQ, D = 512, 1024
NBLK = SEQ // P
GROUPS = ((0, 1), (2, 3))
GMAX = max(len(g) for g in GROUPS)
DC = D // P
H, NOPE, ROPE, VD = 8, 64, 32, 64
QK = NOPE + ROPE
QR, KVR = 384, 256
RH, RD = 4, 128
MEM = 256
MT = MEM // P
XH, XD = 4, 256
PH, KEYS, TOPK = 8, 128, 16
CW = 256
W_SLOTS = 4
ROWS = 12
UNROLL = 3
BANKS = 5
SUM_BANK = 6
HEAD_STEPS = 2 * TOPK + 1
DVE_PICKS = [k for k in range(TOPK) if k % 2 == 0]
PE_PICKS = [k for k in range(TOPK) if k not in DVE_PICKS]
DVE_ROWS = TOPK + len(DVE_PICKS)
PE_ROWS = len(PE_PICKS)
PE_LAG = 5
EARLY = 8
FINAL_FROM = NBLK * PH - 2
LAG = 2
SCRATCH = 3840
EPS = 1e-6
NEG = -1e30
LOW = -3.0e38
MLA_SCALE = QK ** -0.5
X_SCALE = XD ** -0.5

CONST = {}
_at = 0
for _name, _n in (("ident", P), ("causal", P), ("ret_mask", P), ("iota", TOPK), ("key_decay", RH),
                  ("zeta", RH), ("xi", RH), ("xi2", RH), ("eps", 1), ("ret_cos", NBLK * 64),
                  ("ret_sin", NBLK * 64), ("mla_cos", NBLK * 16), ("mla_sin", NBLK * 16)):
    CONST[_name] = (_at, _at + _n)
    _at += _n
CONST_W = _at

GAINS = {"g_mix": DC, "g_mem": DC, "g_xattn": DC, "g_ffn": DC, "g_q_lora": QR // P, "g_kv_lora": KVR // P,
         "g_ret_gn": RH * RD // P}


def constants():
    f = np.float32
    c = np.zeros((P, CONST_W), f)

    def put(name, value):
        a, b = CONST[name]
        c[:, a:b] = value

    i = np.arange(P)
    put("ident", np.eye(P, dtype=f))
    put("causal", np.where(i[None, :] <= i[:, None], f(0), f(NEG)))
    put("ret_mask", np.where(i[None, :] >= i[:, None], f(1), f(0)))
    put("iota", np.arange(TOPK, dtype=f)[None, :])
    gamma = 1.0 - 2.0 ** (-5.0 - np.arange(RH))
    scale = RD ** -0.5
    put("key_decay", scale * gamma[None, :] ** -(i[:, None] + 1.0))
    put("zeta", scale * gamma[None, :] ** (P - 1.0 - i[:, None]))
    put("xi", gamma[None, :] ** (i[:, None] + 1.0))
    put("xi2", gamma[None, :] ** (2 * (i[:, None] + 1.0)))
    put("eps", EPS)
    pos = np.arange(SEQ, dtype=f)
    for name, dim in (("ret", RD), ("mla", ROPE)):
        inv = f(1) / (f(10000.0) ** (np.arange(0, dim, 2, dtype=f) / f(dim)))
        ang = (pos[:, None] * inv[None, :]).astype(f).reshape(NBLK, P, dim // 2).transpose(1, 0, 2)
        put(name + "_cos", np.cos(ang).reshape(P, -1))
        put(name + "_sin", np.sin(ang).reshape(P, -1))
    return c


def chunk_list():
    out = []
    for g in range(len(GROUPS)):
        out += [(g, "in", c) for c in range(3)]
        memory = [(g, kind, h) for h in range(XH) for kind in ("xk", "xv")] if g == 0 else []
        out += memory[:1] + [(g, "uq", 0), (g, "uq", 1), (g, "ukv", 0)] + memory[1:]
        for h in range(RH):
            out += [(g, "qk", h), (g, "vg", h)]
        out += [(g, "o", c) for c in range(4)]
        out += [(g, "xq", h) for h in range(XH)] + [(g, "xo", c) for c in range(4)]
        out += [(g, "pq", h) for h in range(PH)]
    return out


def norm_list():
    out = []
    for g, blocks in enumerate(GROUPS):
        out += [("mix", b) for b in blocks]
        if g == 0:
            out += [("mem", m) for m in range(MT)]
        out += [("x", b) for b in blocks] + [("ffn", b) for b in blocks]
    return out + [("fin", b) for b in range(NBLK)]


def nth(item, b, items):
    blocks = next(g for g in GROUPS if b in g)
    return items * blocks[0] + item * len(blocks) + b - blocks[0] + 1


SHARES = {"mp": 1.3, "pre": 2.0, "mla": 1.6, "ret": 2.0, "gap": 1.5, "add": 2.6, "x": 2.0, "choose": 1.1, "late": 2.0}


LATE = (0, 1, 2, 3, 5, 7, 9, 11)
assert UNROLL * 2 * TOPK % ROWS == 0
assert all(len(g) == 2 for g in GROUPS)


class Head:

    def __init__(self, at, turn=0):
        self.at, self.turn = at, turn

    def times(self, per_head, more):
        return self.turn * (UNROLL * per_head) + (self.at * per_head + more)

    def slot(self, row):
        return (self.at * 2 * TOPK + row) % ROWS

    def landed(self, row):
        return self.turn * (16 * UNROLL * 2 * TOPK // ROWS) + 16 * ((self.at * 2 * TOPK + row) // ROWS + 1)


def in_loops(eng, first, last, body):
    turns = (last - first) // UNROLL
    if turns > 1:
        with eng.Fori(0, turns) as turn:
            for u in range(UNROLL):
                body(Head(first + u, turn))
        first += turns * UNROLL
    for n in range(first, last):
        body(Head(n))


def places_of(g):
    nb = len(GROUPS[g])
    kinds = (["mp"] * 3 + (["pre"] * 2 + ["mla"] * H) * nb + ["ret"] * (RH * nb) + ["gap"] * 3 + ["add"] * 4
             + ["gap"] + ["x"] * (XH * nb) + ["gap"] + ["add"] * 4 + ["gap"] * 2 + ["choose"] * (4 * PH))
    return kinds + ["late"] * PH if g == len(GROUPS) - 1 else kinds


def step_plan():
    places = [[(g, i, SHARES[kind]) for i, kind in enumerate(places_of(g))] for g in range(len(GROUPS))]
    starts = [places_of(g).index("choose") + 3 for g in range(len(GROUPS))]
    plan = {(g, i): range(0) for of_group in places for g, i, _ in of_group}
    for g, blocks in enumerate(GROUPS):
        heads = PH * len(blocks)
        where = places[g][starts[g]:]
        if g + 1 < len(GROUPS):
            where = where + places[g + 1][:starts[g + 1]]
        else:
            heads = EARLY
        total = heads * HEAD_STEPS
        first = blocks[0] * PH * HEAD_STEPS
        whole, seen, done = sum(share for *_, share in where), 0.0, 0
        for gg, i, share in where:
            seen += share
            upto = round(total * seen / whole)
            plan[(gg, i)] = range(first + done, first + upto)
            done = upto
    return plan


def late_plan():
    last = len(GROUPS) - 1
    out = {(g + 1, i): (h, GROUPS[g][1]) for g in range(last) for h, i in enumerate(LATE)}
    first = places_of(last).index("late")
    out.update({(last, first + h): (h, GROUPS[last][1]) for h in range(PH)})
    return out


class Signal:

    def __init__(self, sem):
        self.sem, self.n = sem, 0


class Tile:

    def __init__(self, ap, full, free, use):
        self.ap, self.full, self.free = ap, (full, use), (free, use)


def build_trunk(nc, t, out, consts):
    chunks = chunk_list()
    chunk_no = {key: n for n, key in enumerate(chunks)}
    norms = norm_list()
    norm_no = {key: n for n, key in enumerate(norms)}
    plan = step_plan()
    late = late_plan()
    loop_from = GROUPS[-1][0] * PH + EARLY

    with ExitStack() as ctx:
        def sb(name, shape, dt=F32):
            return ctx.enter_context(nc.sbuf_tensor(name, shape, dt))

        def sem(name):
            return ctx.enter_context(nc.semaphore(name))

        banks = [ctx.enter_context(nc.psum_tensor(f"bank{k}", [P, 512], F32)) for k in range(8)]

        cst = sb("cst", [P, CONST_W])
        h_sb = sb("h_sb", [P, NBLK, D])
        t_cur = sb("t_cur", [P, D])
        g_rows = sb("g_rows", [P, D])
        g_cols = sb("g_cols", [P, len(GAINS), DC])
        w_ring = sb("w_ring", [P, W_SLOTS, DC * CW])
        rows = sb("rows", [P, ROWS, D])
        k_mla = sb("k_mla", [QK, H, SEQ])
        v_mla = sb("v_mla", [P, NBLK, H, VD])
        r_state = sb("r_state", [P, RH, RD])
        xk = sb("xk", [P, 2 * XH, MEM])
        xv = sb("xv", [P, MT, D])
        sk = sb("sk", [P, 2, KEYS])
        expert = sb("expert", [P, NBLK * PH, TOPK], U32)
        gate = sb("gate", [P, NBLK * PH, TOPK])
        mem_rows = rows[:, 2:2 + MT, :]
        mem_t = rows[:, 2 + MT:4 + MT, :].rearrange("p a (c n) -> p (a c) n", n=MEM)
        stage_u = sb("stage_u", [P, TOPK], U32)
        stage_v = sb("stage_v", [P, TOPK], U32)
        diag = sb("diag", [P, PE_ROWS, P])
        dots = sb("dots", [P, TOPK])
        acts = sb("acts", [P, TOPK])
        pick_w = sb("pick_w", [P, TOPK])
        ssq = sb("ssq", [P, len(norms)])
        std = sb("std", [P, len(norms)])
        rstd = sb("rstd", [P, len(norms)])
        a_t = sb("a_t", [P, DC, GMAX * P])
        mix = sb("mix", [P, GMAX, D])
        probs = sb("probs", [P, LAG + 1, 512])
        probs_t = sb("probs_t", [P, 2, 512])
        top = sb("top", [P, LAG + 1])
        mx = sb("mx", [P, 1])
        den = sb("den", [P, 8])
        rden = sb("rden", [P, 8])
        lora = sb("lora", [P, 2, 3])
        gn = sb("gn", [P, GMAX, RH, 2])
        gn_s = sb("gn_s", [P, 4, RH])
        gn_stats = sb("gn_stats", [P, 6])
        scratch = sb("scratch", [P, SCRATCH])

        at = [0]

        def cut(*shape):
            n = int(np.prod(shape))
            ap = scratch[:, at[0]:at[0] + n]
            at[0] += n
            assert at[0] <= SCRATCH
            names = "abc"[:len(shape)]
            if len(shape) == 1:
                return ap
            return ap.rearrange(f"p ({' '.join(names)}) -> p {' '.join(names)}",
                                **dict(zip(names, shape)))

        mp = cut(GMAX, QR + KVR + ROPE)
        lora_t = cut(5, P)
        k_cat = cut(H, QK)
        q_cat = cut(H, QK)
        q_t = scratch[:, GMAX * (QR + KVR + ROPE):][:, 0:H * P].rearrange("p (h n) -> p h n", h=H)
        rot_a, rot_b = probs_t[:, 0, 0:256], probs_t[:, 1, 0:256]
        kpe = sb("kpe", [P, ROPE])
        at[0] = 0
        ret_in = cut(3, 4 * RD)
        ret_qk = cut(3, 2 * RD)
        ret_qk_t = cut(2, 2 * RD)
        ret_s = cut(2, RD)
        ret_kz = cut(2, RD)
        ret_gate = cut(3, RD)
        ret_e = cut(RD)
        at[0] = 0
        xq_t = cut(2, 2, GMAX * P)
        rest = cut(2, KEYS)
        square = cut(D)
        key_s = sb("key_s", [P, 1 + PH, 2, TOPK])
        key_i = sb("key_i", [P, 1 + PH, 2, TOPK], U32)
        hit = sb("hit", [P, 2, TOPK, TOPK])
        cand = hit[:, 0, :, :]
        best = sb("best", [P, TOPK])
        soft = sb("soft", [P, TOPK])
        picked = sb("picked", [P, 2, TOPK])
        small = sb("small", [P, 8])
        best_c = sb("best_c", [P, TOPK], U32)
        split = sb("split", [P, 2, TOPK], U32)

        def const(name):
            a, b = CONST[name]
            return cst[:, a:b]

        ident = const("ident")
        eps = const("eps")

        const_in = sem("const_in")
        g_mix_in = sem("g_mix_in")
        gains_in = sem("gains_in")
        sub_in = sem("sub_in")
        mem_in = sem("mem_in")
        g_rows_in = sem("g_rows_in")
        x_in = [sem(f"x_in{b}") for b in range(NBLK)]
        w_in_slot = [sem(f"w_in_slot{s}") for s in range(W_SLOTS)]
        row_in = [sem(f"row_in{s}") for s in range(ROWS)]
        out_done = sem("out_done")
        bank_full = [sem(f"bank_full{k}") for k in range(8)]
        bank_free = [sem(f"bank_free{k}") for k in range(8)]
        act_step = Signal(sem("act_step"))
        dve_step = Signal(sem("dve_step"))
        std_ready = Signal(sem("std_ready"))
        normed = Signal(sem("normed"))
        lora_std = Signal(sem("lora_std"))
        lora_normed = Signal(sem("lora_normed"))
        q_roped = Signal(sem("q_roped"))
        k_joined = Signal(sem("k_joined"))
        mla_top = Signal(sem("mla_top"))
        mla_out = Signal(sem("mla_out"))
        ret_roped = Signal(sem("ret_roped"))
        ret_exp = Signal(sem("ret_exp"))
        ret_gated = Signal(sem("ret_gated"))
        ret_kz_ready = Signal(sem("ret_kz_ready"))
        ret_s_ready = Signal(sem("ret_s_ready"))
        r_ready = Signal(sem("r_ready"))
        gn_var = Signal(sem("gn_var"))
        gn_std = Signal(sem("gn_std"))
        mixed = Signal(sem("mixed"))
        mix_added = Signal(sem("mix_added"))
        x_top = Signal(sem("x_top"))
        x_out = Signal(sem("x_out"))
        x_added = Signal(sem("x_added"))
        best_ready = Signal(sem("best_ready"))
        soft_ready = Signal(sem("soft_ready"))
        expert_ready = Signal(sem("expert_ready"))
        stage_step = sem("stage_step")
        dve_used = sem("dve_used")
        pe_used = sem("pe_used")
        diag_ready = sem("diag_ready")
        sum_taken = Signal(sem("sum_taken"))
        row_claimed = sem("row_claimed")
        gelu_ready = sem("gelu_ready")
        weights_ready = sem("weights_ready")
        t_ready = Signal(sem("t_ready"))
        out_ready = Signal(sem("out_ready"))

        tiles = {}
        uses = [0] * 8
        turn = [0]
        chunk_freed = {}

        def tile(*name):
            return tiles[name]

        block = ctx.enter_context(nc.Block())

        @block.tensor
        def _(pe):
            def open_tile(name, long_lived=False):
                if long_lived:
                    k = BANKS
                else:
                    k = turn[0] % BANKS
                    turn[0] += 1
                if uses[k]:
                    pe.wait_ge(bank_free[k], uses[k])
                uses[k] += 1
                tiles[name] = Tile(banks[k], bank_full[k], bank_free[k], uses[k])
                return tiles[name]

            def expert_step(head, step, start=False, stop=False):
                k = step - TOPK - 1
                if k not in PE_PICKS:
                    return
                nth_pick = PE_PICKS.index(k)
                s = head.slot(TOPK + k)
                pe.wait_ge(diag_ready, head.times(PE_ROWS, nth_pick + 1))
                pe.wait_ge(row_in[s], head.landed(TOPK + k))
                for i in range(2):
                    ins = pe.matmul(banks[SUM_BANK + i][:, :], diag[:, nth_pick, :],
                                    rows[:, s, i * 512:(i + 1) * 512], start=start, stop=stop)
                ins.then_inc(pe_used, 1)

            place = [0]
            later = []

            def experts(steps):
                for at_step in steps:
                    n, step = divmod(at_step, HEAD_STEPS)
                    start = n % PH == 0 and step == TOPK + 1 + PE_PICKS[0]
                    if start and n:
                        pe.wait_ge(sum_taken.sem, n // PH)
                    expert_step(Head(n), step, start, n % PH == PH - 1 and step == 2 * TOPK)

            def hook(g):
                later.extend(plan[(g, place[0])])
                ends = any((at_step + 1) % (PH * HEAD_STEPS) == 0 for at_step in later)
                now = len(later) if ends else max(0, len(later) - PE_LAG)
                experts(later[:now])
                del later[:now]
                place[0] = place[0] + 1 if (g, place[0] + 1) in plan else 0

            def turn_over(tl, src, n, rows_out=P):
                for i in range(n):
                    ins = pe.transpose(tl.ap[0:rows_out, i * P:(i + 1) * P], src(i), ident)
                ins.then_inc(tl.full[0], 1)

            def weights(g, kind, n):
                no = chunk_no[(g, kind, n)]
                slot, use = no % W_SLOTS, no // W_SLOTS
                pe.wait_ge(w_in_slot[slot], 32 * (use + 1))
                return w_ring[:, slot, :].rearrange("p (c n) -> p c n", c=DC)

            def release(g, kind, n, tl):
                chunk_freed[(g, kind, n)] = tl.full

            def left_operand(kind, blocks, done, value):
                for j, b in enumerate(blocks):
                    pe.wait_ge(done.sem, value(b))
                    for i in range(2):
                        tl = open_tile((kind, b, i))
                        turn_over(tl, lambda c: mix[:, j, (4 * i + c) * P:(4 * i + c + 1) * P], 4)

            def left_ready(src, b):
                for i in range(2):
                    pe.wait_ge(*tile(src, b, i).free)

            def rows_product(g, kind, n, width, blocks, tag, src):
                w = weights(g, kind, n)
                for j, b in enumerate(blocks):
                    if n == 0:
                        left_ready(src, b)
                    tl = open_tile((tag, n, b))
                    for c in range(DC):
                        ins = pe.matmul(tl.ap[:, 0:width], a_t[:, c, j * P:(j + 1) * P], w[:, c, 0:width],
                                        start=c == 0, stop=c == DC - 1)
                    ins.then_inc(tl.full[0], 1)
                release(g, kind, n, tl)

            def columns_product(g, kind, n, blocks, tag, src):
                w = weights(g, kind, n)
                if n == 0:
                    for b in blocks:
                        left_ready(src, b)
                for i in range(2):
                    tl = open_tile((tag, n, i))
                    for c in range(DC):
                        ins = pe.matmul(tl.ap[:, 0:len(blocks) * P], w[:, c, i * P:(i + 1) * P],
                                        a_t[:, c, 0:len(blocks) * P], start=c == 0, stop=c == DC - 1)
                    ins.then_inc(tl.full[0], 1)
                release(g, kind, n, tl)

            def memory_product(n):
                h = n // 2
                if n == 0:
                    for m in range(MT):
                        pe.wait_ge(*tile("mem_t", m, 1).free)
                if n % 2 == 0:
                    w = weights(0, "xk", h)
                    for i in range(2):
                        tl = open_tile(("xk", h, i))
                        for c in range(DC):
                            ins = pe.matmul(tl.ap[:, 0:MEM], w[:, c, i * P:(i + 1) * P], mem_t[:, c, :],
                                            start=c == 0, stop=c == DC - 1)
                        ins.then_inc(tl.full[0], 1)
                    release(0, "xk", h, tl)
                else:
                    w = weights(0, "xv", h)
                    for m in range(MT):
                        tl = open_tile(("xv", h, m))
                        for c in range(DC):
                            ins = pe.matmul(tl.ap[:, 0:CW], mem_t[:, c, m * P:(m + 1) * P], w[:, c, :],
                                            start=c == 0, stop=c == DC - 1)
                        ins.then_inc(tl.full[0], 1)
                    release(0, "xv", h, tl)

            pe.wait_ge(const_in, 16)
            for g, blocks in enumerate(GROUPS):
                left_operand("mix_t", blocks, normed, lambda b: norm_no[("mix", b)] + 1)
                for c in range(3):
                    rows_product(g, "in", c, CW if c < 2 else QR + KVR + ROPE - 2 * CW, blocks, "mp", "mix_t")
                    hook(g)

                if g == 0:
                    pe.wait_ge(sub_in, 16)
                    tl = open_tile(("sk",))
                    turn_over(tl, lambda p: rows[:, 1, p * P:(p + 1) * P], 2)
                    for m in range(MT):
                        pe.wait_ge(normed.sem, norm_no[("mem", m)] + 1)
                        for i in range(2):
                            tl = open_tile(("mem_t", m, i))
                            turn_over(tl, lambda c: mem_rows[:, m, (4 * i + c) * P:(4 * i + c + 1) * P], 4)

                for j, b in enumerate(blocks):
                    if g == 0:
                        memory_product(j)
                    pe.wait_ge(lora_normed.sem, b + 1)
                    for i, n in ((0, 3), (1, 2)):
                        tl = open_tile(("lora_t", b, i))
                        turn_over(tl, lambda c: mp[:, j, (3 * i + c) * P:(3 * i + c + 1) * P], n)
                    for i in range(2):
                        no = chunk_no[(g, "uq", i)]
                        pe.wait_ge(w_in_slot[no % W_SLOTS], 32 * (no // W_SLOTS + 1))
                        w = w_ring[:, no % W_SLOTS, 0:3 * 384].rearrange("p (c n) -> p c n", c=3)
                        if i == 0:
                            pe.wait_ge(*tile("lora_t", b, 0).free)
                        tl = open_tile(("q", b, i))
                        for c in range(3):
                            ins = pe.matmul(tl.ap[:, 0:384], lora_t[:, c, :], w[:, c, :], start=c == 0, stop=c == 2)
                        ins.then_inc(tl.full[0], 1)
                        release(g, "uq", i, tl)
                    no = chunk_no[(g, "ukv", 0)]
                    pe.wait_ge(w_in_slot[no % W_SLOTS], 32 * (no // W_SLOTS + 1))
                    w = w_ring[:, no % W_SLOTS, :].rearrange("p (c n) -> p c n", c=2)
                    pe.wait_ge(*tile("lora_t", b, 1).free)
                    for i in range(2):
                        tl = open_tile(("kv", b, i))
                        for c in range(2):
                            ins = pe.matmul(tl.ap[:, :], lora_t[:, 3 + c, :], w[:, c, i * 512:(i + 1) * 512],
                                            start=c == 0, stop=c == 1)
                        ins.then_inc(tl.full[0], 1)
                    release(g, "ukv", 0, tl)
                    hook(g)
                    pe.wait_ge(k_joined.sem, b + 1)
                    for i in range(2):
                        tl = open_tile(("k_t", b, i))
                        turn_over(tl, lambda c: k_cat[:, 4 * i + c, :], 4, QK)
                    pe.wait_ge(q_roped.sem, b + 1)
                    for i in range(2):
                        tl = open_tile(("q_t", b, i))
                        turn_over(tl, lambda c: q_cat[:, 4 * i + c, :], 4, QK)
                    hook(g)
                    to = open_tile(("o", b), long_lived=True)
                    for h in range(H + LAG + 1):
                        if h < H:
                            if h % 4 == 0:
                                pe.wait_ge(*tile("k_t", b, h // 4).free)
                                pe.wait_ge(*tile("q_t", b, h // 4).free)
                            tl = open_tile(("s", b, h))
                            pe.matmul(tl.ap[:, 0:(b + 1) * P], q_t[0:QK, h, :], k_mla[:, h, 0:(b + 1) * P],
                                      start=True, stop=True).then_inc(tl.full[0], 1)
                        if LAG <= h < H + LAG:
                            i = h - LAG
                            pe.wait_ge(*tile("s", b, i).free)
                            tl = open_tile(("p_t", b, i))
                            turn_over(tl, lambda c: probs[:, i % (LAG + 1), c * P:(c + 1) * P], b + 1)
                        if g == 0 and b == blocks[-1] and h < 2 * XH - 2:
                            memory_product(h + 2)
                        if h > LAG:
                            i = h - LAG - 1
                            pe.wait_ge(*tile("p_t", b, i).free)
                            for c in range(b + 1):
                                ins = pe.matmul(to.ap[:, i * VD:(i + 1) * VD], probs_t[:, i % 2, c * P:(c + 1) * P],
                                                v_mla[:, c, i, :], start=c == 0, stop=c == b)
                            if i == H - 1:
                                ins.then_inc(to.full[0], 1)
                        if h < H:
                            hook(g)

                items = [(h, b) for h in range(RH) for b in blocks]
                for n in range(len(items) + 2):
                    if n < len(items):
                        h, b = items[n]
                        j = b - blocks[0]
                        tl = open_tile(("r", h, b))
                        for half, kind in enumerate(("qk", "vg")):
                            w = weights(g, kind, h)
                            for c in range(DC):
                                ins = pe.matmul(tl.ap[:, half * CW:(half + 1) * CW], a_t[:, c, j * P:(j + 1) * P],
                                                w[:, c, :], start=c == 0, stop=c == DC - 1)
                            release(g, kind, h, tl)
                        ins.then_inc(tl.full[0], 1)
                    if 1 <= n <= len(items):
                        h, b = items[n - 1]
                        k = (n - 1) % 3
                        pe.wait_ge(ret_roped.sem, nth(h, b, RH))
                        tl = open_tile(("r_t", h, b))
                        turn_over(tl, lambda i: ret_qk[:, k, i * RD:(i + 1) * RD], 2)
                    if n >= 2:
                        h, b = items[n - 2]
                        k = (n - 2) % 3
                        pe.wait_ge(ret_s_ready.sem, nth(h, b, RH))
                        m = n % 2
                        tl = open_tile(("r_o", h, b))
                        ins = pe.matmul(tl.ap[:, 0:RD], ret_s[:, m, :], ret_in[:, k, 2 * RD:3 * RD],
                                        start=True, stop=b == 0)
                        if b:
                            pe.wait_ge(r_ready.sem, r_count(h, b - 1))
                            ins = pe.matmul(tl.ap[:, 0:RD], ret_qk_t[:, m, 0:RD], r_state[:, h, :],
                                            start=False, stop=True)
                        ins.then_inc(tl.full[0], 1)
                        if b < NBLK - 1:
                            pe.wait_ge(ret_kz_ready.sem, nth(h, b, RH))
                            tl = open_tile(("r_kv", h, b))
                            pe.matmul(tl.ap[:, 0:RD], ret_kz[:, m, :], ret_in[:, k, 2 * RD:3 * RD],
                                      start=True, stop=True).then_inc(tl.full[0], 1)
                    if 1 <= n <= len(items):
                        h, b = items[n - 1]
                        m = (n - 1) % 2
                        pe.wait_ge(*tile("r_t", h, b).free)
                        tl = open_tile(("r_s", h, b))
                        pe.matmul(tl.ap[:, 0:P], ret_qk_t[:, m, RD:2 * RD], ret_qk_t[:, m, 0:RD],
                                  start=True, stop=True).then_inc(tl.full[0], 1)
                    hook(g)

                left_operand("out_t", blocks, mixed, lambda b: b + 1)
                hook(g)
                for c in range(4):
                    rows_product(g, "o", c, CW, blocks, "wo", "out_t")
                    hook(g)

                left_operand("x_t", blocks, normed, lambda b: norm_no[("x", b)] + 1)
                hook(g)
                items = [(h, b) for h in range(XH) for b in blocks]
                for n in range(len(items) + LAG + 1):
                    if n < len(items):
                        h, b = items[n]
                        j = b - blocks[0]
                        if j == 0:
                            columns_product(g, "xq", h, blocks, ("xq", g), "x_t")
                            pe.wait_ge(*tile(("xq", g), h, 0).free)
                            pe.wait_ge(*tile(("xq", g), h, 1).free)
                        tl = open_tile(("xs", h, b))
                        for i in range(2):
                            ins = pe.matmul(tl.ap[:, 0:MEM], xq_t[:, h % 2, i, j * P:(j + 1) * P], xk[:, 2 * h + i, :],
                                            start=i == 0, stop=i == 1)
                        ins.then_inc(tl.full[0], 1)
                    if LAG <= n < len(items) + LAG:
                        i = n - LAG
                        h, b = items[i]
                        pe.wait_ge(*tile("xs", h, b).free)
                        tl = open_tile(("xp_t", h, b))
                        turn_over(tl, lambda c: probs[:, i % (LAG + 1), c * P:(c + 1) * P], MT)
                    if n > LAG:
                        i = n - LAG - 1
                        h, b = items[i]
                        pe.wait_ge(*tile("xp_t", h, b).free)
                        tl = open_tile(("xo", h, b))
                        for m in range(MT):
                            ins = pe.matmul(tl.ap[:, 0:XD], probs_t[:, i % 2, m * P:(m + 1) * P],
                                            xv[:, m, h * XD:(h + 1) * XD], start=m == 0, stop=m == MT - 1)
                        ins.then_inc(tl.full[0], 1)
                    if n < len(items):
                        hook(g)
                left_operand("xo_t", blocks, x_out, lambda b: nth(XH - 1, b, XH))
                hook(g)
                for c in range(4):
                    rows_product(g, "xo", c, CW, blocks, "wxo", "xo_t")
                    hook(g)

                left_operand("f_t", blocks, normed, lambda b: norm_no[("ffn", b)] + 1)
                hook(g)
                for h in range(PH + 1):
                    if h < PH:
                        columns_product(g, "pq", h, blocks, ("pq", g), "f_t")
                        if h == 0:
                            hook(g)
                    if h >= 1:
                        for i in range(2):
                            pe.wait_ge(*tile(("pq", g), h - 1, i).free)
                        for j, b in enumerate(blocks):
                            tl = open_tile(("ps", h - 1, b))
                            for i in range(2):
                                ins = pe.matmul(tl.ap[:, i * KEYS:(i + 1) * KEYS],
                                                xq_t[:, (h - 1) % 2, i, j * P:(j + 1) * P], sk[:, i, :],
                                                start=True, stop=True)
                            ins.then_inc(tl.full[0], 1)
                            for _ in range(1 if j else 3):
                                hook(g)

            for _ in range(PH):
                hook(len(GROUPS) - 1)
            experts(later)
            for b in GROUPS[-1]:
                if loop_from >= (b + 1) * PH:
                    continue
                first, last = max(loop_from, b * PH), (b + 1) * PH - 1
                if first % PH == 0:
                    experts(range(first * HEAD_STEPS, (first + 1) * HEAD_STEPS))
                    first += 1

                def head_steps(head):
                    for step in range(HEAD_STEPS):
                        expert_step(head, step)

                in_loops(pe, first, last, head_steps)
                experts(range(last * HEAD_STEPS, (last + 1) * HEAD_STEPS))

        @block.sync
        def _(sp):
            def rows_of(gain):
                return gain.rearrange("(a n) -> a n", a=1)

            sp.dma_start(h_sb[:, 0, :], t["x"][0, 0:P, :]).then_inc(x_in[0], 16)
            sp.dma_start(cst[:, :], consts).then_inc(const_in, 16)

            def gain(name, signal):
                n = list(GAINS).index(name)
                sp.dma_start(g_cols[:, n, 0:GAINS[name]], t[name][0].rearrange("(c p) -> p c", p=P),
                             allow_slow_non_contiguous=True).then_inc(signal, 16)

            gain("g_mix", g_mix_in)
            for b in GROUPS[0][1:]:
                sp.dma_start(h_sb[:, b, :], t["x"][0, b * P:(b + 1) * P, :]).then_inc(x_in[b], 16)

            def load_chunk(no):
                g, kind, n = chunks[no]
                slot = no % W_SLOTS
                if no >= W_SLOTS:
                    sp.wait_ge(*chunk_freed[chunks[no - W_SLOTS]])
                dst = w_ring[:, slot, :].rearrange("p (c n) -> p c n", c=DC)
                if kind == "uq":
                    w = t["w_uq"][0].rearrange("(c p) n -> p c n", p=P)
                    dst = w_ring[:, slot, 0:3 * 384].rearrange("p (c n) -> p c n", c=3)
                    parts = [(dst[:, 0:1, :], w[:, 0:1, n * 384:(n + 1) * 384]),
                             (dst[:, 1:3, :], w[:, 1:3, n * 384:(n + 1) * 384])]
                elif kind == "ukv":
                    w = t["w_ukv"][0].rearrange("(c p) n -> p c n", p=P)
                    dst = w_ring[:, slot, :].rearrange("p (c n) -> p c n", c=2)
                    parts = [(dst[:, i, :], w[:, i, :]) for i in range(2)]
                elif kind in ("qk", "vg"):
                    w = t["w_in"][0].rearrange("(c p) n -> p c n", p=P)
                    first = QR + KVR + ROPE + (0 if kind == "qk" else 2 * RH * RD) + n * RD
                    parts = [(dst[:, :, i * RD:(i + 1) * RD],
                              w[:, :, first + i * RH * RD:first + i * RH * RD + RD]) for i in range(2)]
                else:
                    name, first, width = {
                        "in": ("w_in", n * CW, min(CW, QR + KVR + ROPE - n * CW)),
                        "o": ("w_o", n * CW, CW), "xk": ("w_xkv", n * CW, CW),
                        "xv": ("w_xkv", D + n * CW, CW), "xq": ("w_xq", n * CW, CW),
                        "xo": ("w_xo", n * CW, CW), "pq": ("w_pq", n * CW, CW)}[kind]
                    w = t[name][0].rearrange("(c p) n -> p c n", p=P)
                    parts = [(dst[:, i:i + 4, 0:width], w[:, i:i + 4, first:first + width]) for i in (0, 4)]
                for d, s in parts:
                    sp.dma_start(d, s).then_inc(w_in_slot[slot], 16)

            for no in range(W_SLOTS):
                load_chunk(no)
            for m in range(MT):
                sp.dma_start(mem_rows[:, m, :], t["mem"][0, m * P:(m + 1) * P, :]).then_inc(mem_in, 16)
            sp.dma_start(rows[:, 1, 0:2 * P].rearrange("k (p d) -> k p d", p=2),
                         t["sub_keys"][0].rearrange("p k d -> k p d")).then_inc(sub_in, 16)
            for name in list(GAINS)[1:]:
                gain(name, gains_in)
            sp.dma_start(g_rows[:, :], t["g_ffn"][0].partition_broadcast(P)).then_inc(g_rows_in, 16)
            for b in range(len(GROUPS[0]), NBLK):
                sp.dma_start(h_sb[:, b, :], t["x"][0, b * P:(b + 1) * P, :]).then_inc(x_in[b], 16)
            for no in range(W_SLOTS, len(chunks)):
                load_chunk(no)
            sp.wait_ge(t_ready.sem, NBLK)
            sp.dma_start(g_rows[:, :], t["g_final"].partition_broadcast(P)).then_inc(g_rows_in, 16)
            for b in range(NBLK):
                sp.wait_ge(out_ready.sem, b + 1)
                sp.dma_start(out[0, b * P:(b + 1) * P, :], h_sb[:, b, :]).then_inc(out_done, 16)
            sp.wait_ge(out_done, 16 * NBLK)

        @block.scalar
        def _(act):
            def link(ins, sig=act_step):
                ins.then_inc(sig.sem, 1)
                sig.n += 1
                act.wait_ge(sig.sem, sig.n)

            def empty(tl, dst, src):
                nc.scalar.activation(dst, src, ACT.Copy).then_inc(tl.free[0], 1)
                act.wait_ge(*tl.free)

            def square_root(kind, b, src, junk):
                n = norm_no[(kind, b)]
                link(nc.scalar.activation(junk, src, ACT.Square, accum_out=ssq[:, n:n + 1]))
                link(nc.scalar.activation(std[:, n:n + 1], ssq[:, n:n + 1], ACT.Sqrt, bias=eps, scale=1.0 / D),
                     std_ready)

            def empty_scaled(tl, dst, n, gain, first):
                g_no = list(GAINS).index(gain)
                for c in range(n):
                    ins = nc.scalar.activation(dst[:, c, :], tl.ap[:, c * P:(c + 1) * P], ACT.Copy,
                                               scale=g_cols[:, g_no, first + c:first + c + 1])
                    if c < n - 1:
                        ins.then_inc(act_step.sem, 1)
                        act_step.n += 1
                ins.then_inc(tl.free[0], 1)
                act.wait_ge(*tl.free)

            def left_operand(kind, blocks, gain=None):
                for j, b in enumerate(blocks):
                    tl = tile(kind, b, 0)
                    act.wait_ge(*tl.full)
                    dst = a_t[:, 0:4, j * P:(j + 1) * P]
                    if gain is None:
                        empty(tl, dst, tl.ap[:, :].rearrange("p (c n) -> p c n", c=4))
                    else:
                        empty_scaled(tl, dst, 4, gain, 0)

            def expert_step(head, step):
                k = step - TOPK - 1
                if step == TOPK:
                    act.wait_ge(dve_used, head.times(DVE_ROWS, DVE_ROWS + TOPK))
                    nc.scalar.activation(acts[:, :], dots[:, :], ACT.Gelu).then_inc(gelu_ready, 1)
                    act.wait_ge(gelu_ready, head.times(1, 1))
                    act.wait_ge(weights_ready, head.times(1, 1))
                elif k in PE_PICKS:
                    nth_pick = PE_PICKS.index(k)
                    act.wait_ge(pe_used, head.times(PE_ROWS, nth_pick + 1))
                    nc.scalar.activation(diag[:, nth_pick, :], ident, ACT.Copy, scale=pick_w[:, k:k + 1])\
                        .then_inc(diag_ready, 1)

            place = [0]

            def empty_memory(n):
                for i in range(2):
                    tl = tile("xk" if n % 2 == 0 else "xv", n // 2, i)
                    act.wait_ge(*tl.full)
                    if n % 2 == 0:
                        empty(tl, xk[:, n + i, :], tl.ap[:, 0:MEM])
                    else:
                        empty(tl, xv[:, i, n // 2 * XD:(n // 2 + 1) * XD], tl.ap[:, 0:XD])

            def gates(h, b):
                act.wait_ge(best_ready.sem, b * PH + h + 1)
                link(nc.scalar.activation(soft[:, :], best[:, :], ACT.Exp, bias=small[:, 0:1],
                                          accum_out=small[:, 1:2]), soft_ready)

            def hook(g):
                for at_step in plan[(g, place[0])]:
                    n, step = divmod(at_step, HEAD_STEPS)
                    expert_step(Head(n), step)
                if (g, place[0]) in late:
                    gates(*late[(g, place[0])])
                place[0] = place[0] + 1 if (g, place[0] + 1) in plan else 0

            def mix_roots(blocks):
                for b in blocks:
                    act.wait_ge(x_in[b], 16)
                    square_root("mix", b, h_sb[:, b, :], square)

            act.wait_ge(const_in, 16)
            for g, blocks in enumerate(GROUPS):
                nb = len(blocks)
                if g == 0:
                    mix_roots(blocks)
                    act.wait_ge(g_mix_in, 16)
                left_operand("mix_t", blocks, "g_mix")
                if g == 0:
                    act.wait_ge(mem_in, 16 * MT)
                    for m in range(MT):
                        square_root("mem", m, mem_rows[:, m, :], rows[:, 0, :])
                    act.wait_ge(gains_in, 16 * (len(GAINS) - 1))
                if g:
                    act.wait_ge(*tile("ps", PH - 1, GROUPS[g - 1][-1]).free)
                for c in range(3):
                    for j, b in enumerate(blocks):
                        tl = tile("mp", c, b)
                        w = min(CW, QR + KVR + ROPE - c * CW)
                        act.wait_ge(*tl.full)
                        empty(tl, mp[:, j, c * CW:c * CW + w], tl.ap[:, 0:w])
                    hook(g)

                if g == 0:
                    act.wait_ge(*tile("sk").full)
                    empty(tile("sk"), sk[:, :, :], tile("sk").ap[:, 0:2 * P].rearrange("p (c n) -> p c n", c=2))
                    for m in range(MT):
                        for i in range(2):
                            tl = tile("mem_t", m, i)
                            act.wait_ge(*tl.full)
                            empty_scaled(tl, mem_t[:, 4 * i:4 * i + 4, m * P:(m + 1) * P], 4, "g_mem", 4 * i)

                for j, b in enumerate(blocks):
                    if b:
                        act.wait_ge(q_roped.sem, b)
                    link(nc.scalar.activation(probs[:, 0, 0:QR], mp[:, j, 0:QR], ACT.Square,
                                              accum_out=lora[:, 0, 0:1]))
                    link(nc.scalar.activation(probs[:, 0, 0:KVR], mp[:, j, QR:QR + KVR], ACT.Square,
                                              accum_out=lora[:, 1, 0:1]))
                    link(nc.scalar.activation(lora[:, 0, 1:2], lora[:, 0, 0:1], ACT.Sqrt, bias=eps, scale=1.0 / QR))
                    link(nc.scalar.activation(lora[:, 1, 1:2], lora[:, 1, 0:1], ACT.Sqrt, bias=eps, scale=1.0 / KVR),
                         lora_std)
                    if g == 0:
                        empty_memory(j)
                    for i, n in ((0, 3), (1, 2)):
                        tl = tile("lora_t", b, i)
                        act.wait_ge(*tl.full)
                        empty_scaled(tl, lora_t[:, 3 * i:3 * i + n, :], n, "g_kv_lora" if i else "g_q_lora", 0)
                    for i in range(2):
                        tl = tile("q", b, i)
                        act.wait_ge(*tl.full)
                        empty(tl, q_cat[:, 4 * i:4 * i + 4, :], tl.ap[:, 0:4 * QK].rearrange("p (c n) -> p c n", c=4))
                    for i in range(2):
                        tl = tile("kv", b, i)
                        kv = tl.ap[:, :].rearrange("p (c n) -> p c n", c=4)
                        act.wait_ge(*tl.full)
                        link(nc.scalar.activation(k_cat[:, 4 * i:4 * i + 4, 0:NOPE], kv[:, :, 0:NOPE], ACT.Copy))
                        empty(tl, v_mla[:, b, 4 * i:4 * i + 4, :], kv[:, :, NOPE:NOPE + VD])
                    hook(g)
                    for i in range(2):
                        tl = tile("k_t", b, i)
                        act.wait_ge(*tl.full)
                        empty(tl, k_mla[:, 4 * i:4 * i + 4, b * P:(b + 1) * P],
                              tl.ap[0:QK, :].rearrange("p (c n) -> p c n", c=4))
                    for i in range(2):
                        tl = tile("q_t", b, i)
                        act.wait_ge(*tl.full)
                        empty(tl, q_t[0:QK, 4 * i:4 * i + 4, :], tl.ap[0:QK, :].rearrange("p (c n) -> p c n", c=4))
                    hook(g)
                    if b:
                        act.wait_ge(mla_out.sem, b)
                    for h in range(H + LAG):
                        if h < H:
                            tl = tile("s", b, h)
                            act.wait_ge(mla_top.sem, b * H + h + 1)
                            nc.scalar.activation(probs[:, h % (LAG + 1), 0:(b + 1) * P], tl.ap[:, 0:(b + 1) * P],
                                                 ACT.Exp, bias=top[:, h % (LAG + 1):h % (LAG + 1) + 1],
                                                 scale=MLA_SCALE, accum_out=den[:, h:h + 1]).then_inc(tl.free[0], 1)
                            act.wait_ge(*tl.free)
                        if h >= LAG:
                            i = h - LAG
                            tl = tile("p_t", b, i)
                            act.wait_ge(*tl.full)
                            empty(tl, probs_t[:, i % 2, 0:(b + 1) * P], tl.ap[:, 0:(b + 1) * P])
                        if g == 0 and b == blocks[-1] and h < 2 * XH - 2:
                            empty_memory(h + 2)
                        if h < H:
                            hook(g)

                act.wait_ge(mla_out.sem, blocks[-1] + 1)
                items = [(h, b) for h in range(RH) for b in blocks]
                for n in range(len(items) + 2):
                    if n < len(items):
                        h, b = items[n]
                        k = n % 3
                        tl = tile("r", h, b)
                        act.wait_ge(*tl.full)
                        if n >= 3:
                            act.wait_ge(ret_gated.sem, nth(*items[n - 3], RH))
                        empty(tl, ret_in[:, k, :], tl.ap[:, :])
                    if 1 <= n <= len(items):
                        h, b = items[n - 1]
                        k = (n - 1) % 3
                        tl = tile("r_t", h, b)
                        act.wait_ge(*tl.full)
                        empty(tl, ret_qk_t[:, (n - 1) % 2, :], tl.ap[:, 0:2 * RD])
                        act.wait_ge(ret_roped.sem, nth(h, b, RH))
                        z = CONST["zeta"][0] + h
                        link(nc.scalar.activation(ret_kz[:, (n - 1) % 2, :], ret_qk[:, k, RD:], ACT.Copy,
                                                  scale=cst[:, z:z + 1]), ret_kz_ready)
                    if n < len(items):
                        if n >= 1:
                            act.wait_ge(ret_gated.sem, nth(*items[n - 1], RH))
                        link(nc.scalar.activation(ret_e, ret_in[:, n % 3, 3 * RD:], ACT.Exp, scale=-1.0), ret_exp)
                    hook(g)
                for j, b in enumerate(blocks):
                    act.wait_ge(gn_var.sem, b + 1)
                    link(nc.scalar.activation(gn_s[:, 1, :], gn_s[:, 0, :], ACT.Sqrt, bias=eps), gn_std)

                left_operand("out_t", blocks)
                hook(g)
                for c in range(4):
                    hook(g)
                for j, b in enumerate(blocks):
                    act.wait_ge(mix_added.sem, nth(3, b, 4))
                    act.wait_ge(*tile("out_t", b, 1).full)
                    square_root("x", b, h_sb[:, b, :], mix[:, j, :])
                left_operand("x_t", blocks, "g_xattn")
                hook(g)
                items = [(h, b) for h in range(XH) for b in blocks]
                for n in range(len(items) + LAG):
                    if n < len(items):
                        h, b = items[n]
                        if b == blocks[0]:
                            for i in range(2):
                                tl = tile(("xq", g), h, i)
                                act.wait_ge(*tl.full)
                                empty(tl, xq_t[:, h % 2, i, 0:nb * P], tl.ap[:, 0:nb * P])
                        tl = tile("xs", h, b)
                        k = n % (LAG + 1)
                        act.wait_ge(x_top.sem, nth(h, b, XH))
                        if n >= 8:
                            act.wait_ge(x_out.sem, nth(*items[n - 8], XH))
                        nc.scalar.activation(probs[:, k, 0:MEM], tl.ap[:, 0:MEM], ACT.Exp, bias=top[:, k:k + 1],
                                             scale=X_SCALE, accum_out=den[:, n % 8:n % 8 + 1]).then_inc(tl.free[0], 1)
                        act.wait_ge(*tl.free)
                    if n >= LAG:
                        h, b = items[n - LAG]
                        tl = tile("xp_t", h, b)
                        act.wait_ge(*tl.full)
                        empty(tl, probs_t[:, (n - LAG) % 2, 0:MEM], tl.ap[:, 0:MEM])
                    if n < len(items):
                        hook(g)
                left_operand("xo_t", blocks)
                hook(g)
                for c in range(4):
                    hook(g)
                for j, b in enumerate(blocks):
                    act.wait_ge(x_added.sem, nth(3, b, 4))
                    act.wait_ge(*tile("xo_t", b, 1).full)
                    square_root("ffn", b, h_sb[:, b, :], mix[:, j, :])

                left_operand("f_t", blocks, "g_ffn")
                if g + 1 < len(GROUPS):
                    mix_roots(GROUPS[g + 1])
                hook(g)
                for h in range(PH + 1):
                    if h < PH:
                        for i in range(2):
                            tl = tile(("pq", g), h, i)
                            act.wait_ge(*tl.full)
                            empty(tl, xq_t[:, h % 2, i, 0:nb * P], tl.ap[:, 0:nb * P])
                        if h == 0:
                            hook(g)
                    if h >= 1:
                        hook(g)
                        gates(h - 1, blocks[0])
                        for _ in range(3):
                            hook(g)
            for _ in range(PH):
                hook(len(GROUPS) - 1)

            def head_steps(head):
                for step in range(HEAD_STEPS):
                    expert_step(head, step)

            def final_root(b):
                act.wait_ge(sum_taken.sem, b + 1)
                square_root("fin", b, h_sb[:, b, :], square)

            in_loops(act, loop_from, FINAL_FROM, head_steps)
            for b in range(NBLK - 1):
                final_root(b)
            in_loops(act, FINAL_FROM, NBLK * PH, head_steps)
            final_root(NBLK - 1)

        @block.vector
        def _(dve):
            def link(ins, sig=dve_step, hold=True):
                ins.then_inc(sig.sem, 1)
                sig.n += 1
                if hold:
                    dve.wait_ge(sig.sem, sig.n)

            def last_read(ins, tl):
                ins.then_inc(tl.free[0], 1)
                dve.wait_ge(*tl.free)

            def norm(kind, b, src, dst, gain=None):
                n = norm_no[(kind, b)]
                dve.wait_ge(std_ready.sem, n + 1)
                link(nc.vector.reciprocal(rstd[:, n:n + 1], std[:, n:n + 1]))
                if gain is None:
                    ins = nc.vector.tensor_scalar(dst, src, rstd[:, n:n + 1], None, ALU.mult)
                else:
                    ins = nc.vector.scalar_tensor_tensor(dst, src, rstd[:, n:n + 1], gain, ALU.mult, ALU.mult)
                ins.then_inc(normed.sem, 1)
                dve.wait_ge(normed.sem, n + 1)

            def left_operand(kind, blocks, gain=None, first=4):
                for j, b in enumerate(blocks):
                    tl = tile(kind, b, 1)
                    dve.wait_ge(*tl.full)
                    for c in range(4):
                        dst, src = a_t[:, 4 + c, j * P:(j + 1) * P], tl.ap[:, c * P:(c + 1) * P]
                        if gain is None:
                            ins = nc.vector.tensor_copy(dst, src)
                        else:
                            column = g_cols[:, list(GAINS).index(gain), first + c:first + c + 1]
                            ins = nc.vector.tensor_scalar(dst, src, column, None, ALU.mult)
                        if c < 3:
                            link(ins, hold=False)
                        else:
                            last_read(ins, tl)

            def rotate(x, dst, cos, sin, n, half, sig):
                a = rot_a[:, 0:n * 2 * half].rearrange("p (n t f) -> p n t f", n=n, t=2)
                b = rot_b[:, 0:n * 2 * half].rearrange("p (n t f) -> p n t f", n=n, t=2)
                c4 = cos.unsqueeze(1).unsqueeze(1).to_broadcast([P, n, 2, half])
                s4 = sin.unsqueeze(1).unsqueeze(1).to_broadcast([P, n, 2, half])
                link(nc.vector.tensor_tensor(a, x, c4, ALU.mult), hold=False)
                link(nc.vector.tensor_tensor(b, x, s4, ALU.mult))
                link(nc.vector.tensor_tensor(dst[:, :, 0, :], a[:, :, 0, :], b[:, :, 1, :], ALU.subtract))
                link(nc.vector.tensor_tensor(dst[:, :, 1, :], b[:, :, 0, :], a[:, :, 1, :], ALU.add), sig)

            def add_product(g, tag, blocks, sig):
                for c in range(4):
                    for b in blocks:
                        tl = tile(tag, c, b)
                        dve.wait_ge(*tl.full)
                        hb = h_sb[:, b, c * CW:(c + 1) * CW]
                        last_read(nc.vector.tensor_tensor(hb, hb, tl.ap[:, 0:CW], ALU.add), tl)
                        dve.sem_inc(sig.sem, 1)
                        sig.n += 1
                    hook(g)

            def expert_step(head, b, step):
                if step < TOPK:
                    s = head.slot(step)
                    dve.wait_ge(row_in[s], head.landed(step))
                    nc.vector.tensor_tensor_reduce(out=rows[:, s, :], in0=rows[:, s, :], in1=t_cur[:, :], scale=1.0,
                                                   scalar=0.0, op0=ALU.mult, op1=ALU.add,
                                                   accum_out=dots[:, step:step + 1]).then_inc(dve_used, 1)
                elif step == TOPK:
                    dve.wait_ge(gelu_ready, head.times(1, 1))
                    if not (isinstance(head.turn, int) and head.at == 0):
                        dve.wait_ge(diag_ready, head.times(PE_ROWS, 0))
                    if isinstance(head.turn, int):
                        g_n = gate[:, head.at, :]
                    else:
                        g_n = gate[:, bass.ds(head.times(1, 0), 1), :].rearrange("p a k -> p (a k)")
                    nc.vector.tensor_tensor(pick_w[:, :], acts[:, :], g_n, ALU.mult).then_inc(weights_ready, 1)
                    dve.wait_ge(weights_ready, head.times(1, 1))
                elif step - TOPK - 1 in DVE_PICKS:
                    k = step - TOPK - 1
                    s = head.slot(TOPK + k)
                    dve.wait_ge(row_in[s], head.landed(TOPK + k))
                    nc.vector.scalar_tensor_tensor(h_sb[:, b, :], rows[:, s, :], pick_w[:, k:k + 1], h_sb[:, b, :],
                                                   ALU.mult, ALU.add).then_inc(dve_used, 1)
                    dve.wait_ge(dve_used, head.times(DVE_ROWS, DVE_ROWS + TOPK + DVE_PICKS.index(k) + 1))

            place = [0]

            def hook(g):
                for at_step in plan[(g, place[0])]:
                    n, step = divmod(at_step, HEAD_STEPS)
                    if step == 0 and n % PH == 0:
                        expert_tokens(n // PH)
                    expert_step(Head(n), n // PH, step)
                if (g, place[0]) in late:
                    h, b = late[(g, place[0])]
                    choose_pairs(h, b, 1 + h)
                place[0] = place[0] + 1 if (g, place[0] + 1) in plan else 0

            def take_sum(b):
                dve.wait_ge(pe_used, PE_ROWS + (b + 1) * PH * PE_ROWS)
                for i in range(2):
                    hb = h_sb[:, b, i * 512:(i + 1) * 512]
                    link(nc.vector.tensor_tensor(hb, hb, banks[SUM_BANK + i][:, :], ALU.add),
                         sum_taken if i else dve_step)

            def expert_tokens(b):
                if b:
                    take_sum(b - 1)
                else:
                    dve.wait_ge(g_rows_in, 16)
                n = norm_no[("ffn", b)]
                link(nc.vector.scalar_tensor_tensor(t_cur[:, :], h_sb[:, b, :], rstd[:, n:n + 1], g_rows[:, :],
                                                    ALU.mult, ALU.mult), t_ready)

            def final_norm(b):
                norm("fin", b, h_sb[:, b, :], h_sb[:, b, :], g_rows[:, :])
                dve.sem_inc(out_ready.sem, 1)

            def choose_keys(h, b, slot):
                tl = tile("ps", h, b)
                dve.wait_ge(*tl.full)
                scores = [tl.ap[:, p * KEYS:(p + 1) * KEYS] for p in range(2)]
                values, places_of = key_s[:, slot, :, :], key_i[:, slot, :, :]
                for p in range(2):
                    link(nc.vector.max(values[:, p, 0:8], scores[p]), hold=p == 1)
                for p in range(2):
                    link(nc.vector.match_replace(rest[:, p, :], values[:, p, 0:8], scores[p], LOW), hold=p == 1)
                for p in range(2):
                    link(nc.vector.max(values[:, p, 8:16], rest[:, p, :]), hold=p == 1)
                for p in range(2):
                    link(nc.vector.max_index(places_of[:, p, 8:16], values[:, p, 8:16], rest[:, p, :]), hold=False)
                link(nc.vector.max_index(places_of[:, 0, 0:8], values[:, 0, 0:8], scores[0]), hold=False)
                last_read(nc.vector.max_index(places_of[:, 1, 0:8], values[:, 1, 0:8], scores[1]), tl)

            def choose_pairs(h, b, slot, between=None):
                values, places_of = key_s[:, slot, :, :], key_i[:, slot, :, :]
                link(nc.vector.tensor_tensor(cand, values[:, 0, :].unsqueeze(2).to_broadcast([P, TOPK, TOPK]),
                                             values[:, 1, :].unsqueeze(1).to_broadcast([P, TOPK, TOPK]), ALU.add))
                pairs = cand.rearrange("p a b -> p (a b)")
                link(nc.vector.max(best[:, 0:8], pairs))
                link(nc.vector.tensor_scalar(small[:, 0:1], best[:, 0:1], -1.0, None, ALU.mult), hold=False)
                link(nc.vector.max_index(best_c[:, 0:8], best[:, 0:8], pairs))
                link(nc.vector.match_replace(pairs, best[:, 0:8], pairs, LOW))
                link(nc.vector.max(best[:, 8:16], pairs), best_ready)
                link(nc.vector.max_index(best_c[:, 8:16], best[:, 8:16], pairs))
                if between:
                    between()
                link(nc.vector.tensor_scalar(split[:, 0, :], best_c[:, :], 4, None, ALU.logical_shift_right),
                     hold=False)
                link(nc.vector.tensor_scalar(split[:, 1, :], best_c[:, :], 15, None, ALU.bitwise_and))
                for p in range(2):
                    link(nc.vector.tensor_tensor(hit[:, p, :, :],
                                                 split[:, p, :].unsqueeze(2).to_broadcast([P, TOPK, TOPK]),
                                                 const("iota").unsqueeze(1).to_broadcast([P, TOPK, TOPK]),
                                                 ALU.is_equal), hold=p == 1)
                for p in range(2):
                    link(nc.vector.tensor_tensor(hit[:, p, :, :], hit[:, p, :, :],
                                                 places_of[:, p, :].unsqueeze(1).to_broadcast([P, TOPK, TOPK]),
                                                 ALU.mult), hold=p == 1)
                link(nc.vector.tensor_reduce(picked[:, :, :], hit[:, :, :, :], AX.X, ALU.add))
                dve.wait_ge(soft_ready.sem, b * PH + h + 1)
                link(nc.vector.reciprocal(small[:, 2:3], small[:, 1:2]))
                link(nc.vector.tensor_scalar(gate[:, b * PH + h, :], soft[:, :], small[:, 2:3], None, ALU.mult))
                link(nc.vector.scalar_tensor_tensor(expert[:, b * PH + h, :], picked[:, 0, :], float(KEYS),
                                                    picked[:, 1, :], ALU.mult, ALU.add), expert_ready)

            dve.sem_inc(dve_used, DVE_ROWS)
            dve.sem_inc(pe_used, PE_ROWS)
            dve.wait_ge(const_in, 16)
            for g, blocks in enumerate(GROUPS):
                nb = len(blocks)
                if g == 0:
                    for j, b in enumerate(blocks):
                        norm("mix", b, h_sb[:, b, :], mix[:, j, :])
                    dve.wait_ge(g_mix_in, 16)
                left_operand("mix_t", blocks, "g_mix")
                if g == 0:
                    for m in range(MT):
                        norm("mem", m, mem_rows[:, m, :], mem_rows[:, m, :])
                for c in range(3):
                    hook(g)

                for j, b in enumerate(blocks):
                    dve.wait_ge(lora_std.sem, b + 1)
                    link(nc.vector.reciprocal(lora[:, :, 2], lora[:, :, 1]))
                    qv, kv = mp[:, j, 0:QR], mp[:, j, QR:QR + KVR]
                    link(nc.vector.tensor_scalar(qv, qv, lora[:, 0, 2:3], None, ALU.mult), hold=False)
                    link(nc.vector.tensor_scalar(kv, kv, lora[:, 1, 2:3], None, ALU.mult), lora_normed)
                    cos = const("mla_cos")[:, b * 16:(b + 1) * 16]
                    sin = const("mla_sin")[:, b * 16:(b + 1) * 16]
                    rotate(mp[:, j, QR + KVR:].rearrange("p (n t f) -> p n t f", n=1, t=2),
                           kpe[:, :].rearrange("p (n t f) -> p n t f", n=1, t=2), cos, sin, 1, 16, dve_step)
                    hook(g)
                    dve.wait_ge(*tile("kv", b, 1).free)
                    link(nc.vector.tensor_copy(k_cat[:, :, NOPE:],
                                               kpe[:, :].unsqueeze(1).to_broadcast([P, H, ROPE])), k_joined)
                    qr = q_cat[:, :, NOPE:].rearrange("p n (t f) -> p n t f", t=2)
                    rotate(qr, qr, cos, sin, H, 16, q_roped)
                    hook(g)
                    for h in range(H):
                        tl = tile("s", b, h)
                        k = h % (LAG + 1)
                        dve.wait_ge(*tl.full)
                        own = tl.ap[:, b * P:(b + 1) * P]
                        link(nc.vector.tensor_tensor(own, own, const("causal"), ALU.add))
                        link(nc.vector.tensor_reduce(mx[:, :], tl.ap[:, 0:(b + 1) * P], AX.X, ALU.max))
                        if h > LAG:
                            dve.wait_ge(*tile("s", b, h - LAG - 1).free)
                        link(nc.vector.tensor_scalar(top[:, k:k + 1], mx[:, :], -MLA_SCALE, None, ALU.mult), mla_top)
                        hook(g)
                    to = tile("o", b)
                    dve.wait_ge(*to.full)
                    link(nc.vector.reciprocal(rden[:, :], den[:, :]))
                    last_read(nc.vector.tensor_tensor(
                        mix[:, j, 0:H * VD].rearrange("p (h d) -> p h d", h=H),
                        to.ap[:, :].rearrange("p (h d) -> p h d", h=H),
                        rden[:, :].unsqueeze(2).to_broadcast([P, H, VD]), ALU.mult), to)
                    dve.sem_inc(mla_out.sem, 1)
                    mla_out.n += 1

                items = [(h, b) for h in range(RH) for b in blocks]
                for n in range(len(items) + 2):
                    if n < len(items):
                        h, b = items[n]
                        k = n % 3
                        dve.wait_ge(*tile("r", h, b).free)
                        rotate(ret_in[:, k, 0:2 * RD].rearrange("p (n t f) -> p n t f", n=2, t=2),
                               ret_qk[:, k, :].rearrange("p (n t f) -> p n t f", n=2, t=2),
                               const("ret_cos")[:, b * 64:(b + 1) * 64], const("ret_sin")[:, b * 64:(b + 1) * 64],
                               2, 64, ret_roped)
                        dve.wait_ge(ret_exp.sem, nth(h, b, RH))
                        link(nc.vector.tensor_scalar(ret_e, ret_e, 1.0, None, ALU.add))
                        link(nc.vector.reciprocal(ret_e, ret_e))
                        link(nc.vector.tensor_tensor(ret_gate[:, k, :], ret_e, ret_in[:, k, 3 * RD:], ALU.mult),
                             ret_gated)
                    hook(g)
                    if n >= 2:
                        h, b = items[n - 2]
                        k = (n - 2) % 3
                        j = b - blocks[0]
                        tl = tile("r_o", h, b)
                        dve.wait_ge(*tl.full)
                        link(nc.vector.bn_stats(gn_stats[:, :], tl.ap[:, 0:RD]))
                        link(nc.vector.bn_aggr(gn[:, j, h, :], gn_stats[:, :]))
                        last_read(nc.vector.scalar_tensor_tensor(
                            mix[:, j, H * VD + h * RD:H * VD + (h + 1) * RD], tl.ap[:, 0:RD], gn[:, j, h, 0:1],
                            ret_gate[:, k, :], ALU.subtract, ALU.mult), tl)
                        if b < NBLK - 1:
                            tl = tile("r_kv", h, b)
                            dve.wait_ge(*tl.full)
                            if b == 0:
                                ins = nc.vector.tensor_copy(r_state[:, h, :], tl.ap[:, 0:RD])
                            else:
                                ins = nc.vector.scalar_tensor_tensor(
                                    r_state[:, h, :], r_state[:, h, :], float((1.0 - 2.0 ** (-5.0 - h)) ** P),
                                    tl.ap[:, 0:RD], ALU.mult, ALU.add)
                            last_read(ins, tl)
                            dve.sem_inc(r_ready.sem, 1)
                            r_ready.n += 1
                    if 1 <= n <= len(items):
                        h, b = items[n - 1]
                        tl = tile("r_s", h, b)
                        dve.wait_ge(*tl.full)
                        z = CONST["key_decay"][0] + h
                        last_read(nc.vector.scalar_tensor_tensor(
                            ret_s[:, (n - 1) % 2, :], tl.ap[:, 0:P], cst[:, z:z + 1], const("ret_mask"),
                            ALU.mult, ALU.mult), tl)
                        dve.sem_inc(ret_s_ready.sem, 1)
                        ret_s_ready.n += 1
                for j, b in enumerate(blocks):
                    link(nc.vector.tensor_tensor(gn_s[:, 0, :], gn[:, j, :, 1], const("xi2"), ALU.mult), gn_var)
                    dve.wait_ge(gn_std.sem, b + 1)
                    link(nc.vector.reciprocal(gn_s[:, 2, :], gn_s[:, 1, :]))
                    link(nc.vector.tensor_tensor(gn_s[:, 3, :], gn_s[:, 2, :], const("xi"), ALU.mult))
                    o = mix[:, j, H * VD:].rearrange("p (h d) -> p h d", h=RH)
                    link(nc.vector.tensor_tensor(o, o, gn_s[:, 3, :].unsqueeze(2).to_broadcast([P, RH, RD]),
                                                 ALU.mult), mixed)
                if g == 0:
                    dve.wait_ge(gains_in, 16 * (len(GAINS) - 1))
                left_operand("out_t", blocks, "g_ret_gn", first=0)
                hook(g)
                add_product(g, "wo", blocks, mix_added)

                for j, b in enumerate(blocks):
                    norm("x", b, h_sb[:, b, :], mix[:, j, :])
                left_operand("x_t", blocks, "g_xattn")
                hook(g)
                for j, b in enumerate(blocks):
                    dve.wait_ge(*tile("x_t", b, 1).full)
                items = [(h, b) for h in range(XH) for b in blocks]
                for n in range(len(items) + LAG + 1):
                    if n < len(items):
                        h, b = items[n]
                        k = n % (LAG + 1)
                        tl = tile("xs", h, b)
                        dve.wait_ge(*tl.full)
                        link(nc.vector.tensor_reduce(mx[:, :], tl.ap[:, 0:MEM], AX.X, ALU.max))
                        if n > LAG:
                            dve.wait_ge(*tile("xs", *items[n - LAG - 1]).free)
                        link(nc.vector.tensor_scalar(top[:, k:k + 1], mx[:, :], -X_SCALE, None, ALU.mult), x_top)
                    if n > LAG:
                        h, b = items[n - LAG - 1]
                        k = (n - LAG - 1) % 8
                        j = b - blocks[0]
                        tl = tile("xo", h, b)
                        dve.wait_ge(*tl.full)
                        link(nc.vector.reciprocal(rden[:, k:k + 1], den[:, k:k + 1]))
                        last_read(nc.vector.tensor_scalar(mix[:, j, h * XD:(h + 1) * XD], tl.ap[:, 0:XD],
                                                          rden[:, k:k + 1], None, ALU.mult), tl)
                        dve.sem_inc(x_out.sem, 1)
                        x_out.n += 1
                    if n < len(items):
                        hook(g)
                left_operand("xo_t", blocks)
                hook(g)
                add_product(g, "wxo", blocks, x_added)

                for j, b in enumerate(blocks):
                    norm("ffn", b, h_sb[:, b, :], mix[:, j, :])
                left_operand("f_t", blocks, "g_ffn")
                hook(g)
                if g + 1 < len(GROUPS):
                    for b in blocks:
                        dve.wait_ge(*tile("f_t", b, 1).full)
                    for j, b in enumerate(GROUPS[g + 1]):
                        norm("mix", b, h_sb[:, b, :], mix[:, j, :])
                hook(g)
                for h in range(PH):
                    choose_keys(h, blocks[0], 0)
                    hook(g)
                    choose_pairs(h, blocks[0], 0, between=lambda: hook(g))
                    hook(g)
                    choose_keys(h, blocks[1], 1 + h)
                    hook(g)
            for _ in range(PH):
                hook(len(GROUPS) - 1)

            for b in GROUPS[-1]:
                if b * PH >= loop_from:
                    expert_tokens(b)

                def head_steps(head):
                    for step in range(HEAD_STEPS):
                        expert_step(head, b, step)

                if b < NBLK - 1:
                    in_loops(dve, max(loop_from, b * PH), (b + 1) * PH, head_steps)
                else:
                    in_loops(dve, b * PH, FINAL_FROM, head_steps)
                    dve.wait_ge(g_rows_in, 32)
                    for done in range(b):
                        final_norm(done)
                    in_loops(dve, FINAL_FROM, NBLK * PH, head_steps)
            take_sum(NBLK - 1)
            final_norm(NBLK - 1)

        @block.gpsimd
        def _(pool):
            def slot_free(head, row):
                at, old = divmod(head.at * 2 * TOPK + row - ROWS, 2 * TOPK)
                before = Head(at, head.turn)
                if old < TOPK:
                    pool.wait_ge(dve_used, before.times(DVE_ROWS, DVE_ROWS + old + 1))
                elif old - TOPK in DVE_PICKS:
                    pool.wait_ge(dve_used, before.times(DVE_ROWS, DVE_ROWS + TOPK + DVE_PICKS.index(old - TOPK) + 1))
                else:
                    pool.wait_ge(pe_used, before.times(PE_ROWS, PE_ROWS + PE_PICKS.index(old - TOPK) + 1))

            def gathers(head):
                if isinstance(head.turn, int):
                    picks = expert[:, head.at, :]
                else:
                    picks = expert[:, bass.ds(head.times(1, 0), 1), :].rearrange("p a k -> p (a k)")
                for kind, (stage, table) in enumerate(((stage_u, t["u_experts"]), (stage_v, t["v_experts"]))):
                    nc.gpsimd.tensor_copy(stage[:, :], picks).then_inc(stage_step, 1)
                    pool.wait_ge(stage_step, head.times(2, kind + 1))
                    for k in range(TOPK):
                        row = kind * TOPK + k
                        s = head.slot(row)
                        slot_free(head, row)
                        pool.sem_inc(row_claimed, 1)
                        nc.gpsimd.indirect_dma_start(
                            rows[:, s, :], None, table[0],
                            bass.IndirectOffsetOnAxis(ap=stage[:, k:k + 1], axis=0)).then_inc(row_in[s], 16)

            def chosen_gathers(head):
                pool.wait_ge(expert_ready.sem, head.times(1, 1))
                gathers(head)

            in_loops(pool, 0, NBLK * PH, chosen_gathers)


def r_count(h, b):
    n = 0
    for blocks in GROUPS:
        for hh in range(RH):
            for bb in blocks:
                if bb < NBLK - 1:
                    n += 1
                    if (hh, bb) == (h, b):
                        return n
    raise ValueError


_INS = ["x", "mem", "g_mix", "w_in", "g_q_lora", "w_uq", "g_kv_lora", "w_ukv", "g_ret_gn", "w_o", "g_xattn", "g_mem",
        "w_xq", "w_xkv", "w_xo", "g_ffn", "w_pq", "sub_keys", "u_experts", "v_experts", "g_final"]


def kernel(**inputs):
    import concourse.bacc as bacc
    from concourse.bass_utils import run_bass_kernel_spmd

    nc = bacc.Bacc("TRN2", target_bir_lowering=False, num_devices=1)
    arrays, t = {}, {}
    for name in _INS:
        a = np.ascontiguousarray(inputs[name])
        arrays[f"in_{name}"] = a
        t[name] = nc.dram_tensor(f"in_{name}", a.shape, mybir.dt.from_np(a.dtype), kind="ExternalInput").ap()
    arrays["in_consts"] = constants()
    consts = nc.dram_tensor("in_consts", (P, CONST_W), F32, kind="ExternalInput").ap()
    out = nc.dram_tensor("out_0", (1, SEQ, D), F32, kind="ExternalOutput").ap()
    build_trunk(nc, t, out, consts)
    r = run_bass_kernel_spmd(nc, [arrays], core_ids=[0])
    return r.results[0]["out_0"]
```
